# Optimizing a Trainium2 kernel written in Bass

```python
import jax, jax.numpy as jnp
from jax import lax
import numpy as np

D_MODEL = 2048
BATCH = 1
SEQ = 512
DEPTH = 2

N_MIXERS = 2
BLOCK = 128
NEG_INF = -1e30
RMS_EPS = 1e-6
FOX_HEAD_DIM = 64
FOX_HEADS = D_MODEL // FOX_HEAD_DIM
FOX_WIDTH = FOX_HEADS * FOX_HEAD_DIM
FOX_IN = 4 * FOX_WIDTH + FOX_HEADS
SWA_HEAD_DIM = 64
SWA_Q_HEADS = D_MODEL // SWA_HEAD_DIM
SWA_KV_HEADS = SWA_Q_HEADS // 8
SWA_GROUP = SWA_Q_HEADS // SWA_KV_HEADS
SWA_WINDOW = 128
SWA_WIDTH = SWA_Q_HEADS * SWA_HEAD_DIM
SWA_KV_WIDTH = SWA_KV_HEADS * SWA_HEAD_DIM
SWA_IN = 2 * SWA_WIDTH + 2 * SWA_KV_WIDTH
ROPE_THETA = 500000.0
ROT_DIM = SWA_HEAD_DIM // 4
N_FOX_LAYERS = (DEPTH + 1) // 2
N_SWA_LAYERS = DEPTH // 2


def rmsnorm(x, g):
    x32 = x.astype(jnp.float32)
    y = x32 * lax.rsqrt(jnp.mean(x32 * x32, axis=-1, keepdims=True) + RMS_EPS)
    return (y * g.astype(jnp.float32)).astype(x.dtype)

def partial_rope(x, pos):
    half = ROT_DIM // 2
    inv_freq = ROPE_THETA ** (-jnp.arange(half, dtype=jnp.float32) / half)
    ang = pos[:, None] * inv_freq[None, :]
    cos = jnp.cos(ang)[None, :, None, :]
    sin = jnp.sin(ang)[None, :, None, :]
    x32 = x.astype(jnp.float32)
    x1, x2 = x32[..., :half], x32[..., half:ROT_DIM]
    rot = jnp.concatenate([x1 * cos - x2 * sin, x2 * cos + x1 * sin], axis=-1)
    return jnp.concatenate([rot.astype(x.dtype), x[..., ROT_DIM:]], axis=-1)

def fox_attention(q, k, v, log_f):
    B, S, H, d = q.shape
    nb = S // BLOCK
    scale = d ** -0.5
    c = jnp.cumsum(log_f, axis=1).transpose(0, 2, 1)
    kf = k.astype(jnp.float32)
    key_pos = jnp.arange(S)
    qb = q.reshape(B, nb, BLOCK, H, d).transpose(1, 0, 2, 3, 4)
    cb = c.reshape(B, H, nb, BLOCK).transpose(2, 0, 1, 3)

    def one_block(args):
        qi, ci, i = args
        s = jnp.einsum('bqhd,bkhd->bhqk', qi.astype(jnp.float32), kf) * scale
        s = s + ci[..., None] - c[:, :, None, :]
        qpos = i * BLOCK + jnp.arange(BLOCK)
        mask = key_pos[None, :] <= qpos[:, None]
        s = jnp.where(mask[None, None], s, NEG_INF)
        p = jax.nn.softmax(s, axis=-1).astype(v.dtype)
        return jnp.einsum('bhqk,bkhd->bqhd', p, v)

    out = lax.map(one_block, (qb, cb, jnp.arange(nb)))
    return out.transpose(1, 0, 2, 3, 4).reshape(B, S, H * d)

def swa_attention(q, k, v, sinks):
    B, S = q.shape[:2]
    nb = S // BLOCK
    scale = SWA_HEAD_DIM ** -0.5
    qb = q.reshape(B, nb, BLOCK, SWA_KV_HEADS, SWA_GROUP, SWA_HEAD_DIM)

    def band(t):
        tp = jnp.pad(t, ((0, 0), (BLOCK, 0), (0, 0), (0, 0)))
        tp = tp.reshape(B, nb + 1, BLOCK, SWA_KV_HEADS, SWA_HEAD_DIM)
        return jnp.concatenate([tp[:, :-1], tp[:, 1:]], axis=2)

    kw, vw = band(k), band(v)
    s = jnp.einsum('bnqhgd,bnkhd->bnhgqk', qb.astype(jnp.float32), kw.astype(jnp.float32)) * scale
    t_loc = jnp.arange(BLOCK)[:, None]
    j_loc = jnp.arange(2 * BLOCK)[None, :]
    diff = t_loc + BLOCK - j_loc
    key_abs = (jnp.arange(nb)[:, None, None] - 1) * BLOCK + j_loc[None]
    mask = (diff >= 0)[None] & (diff < SWA_WINDOW)[None] & (key_abs >= 0)
    s = jnp.where(mask[None, :, None, None], s, NEG_INF)
    sink = sinks.astype(jnp.float32).reshape(SWA_KV_HEADS, SWA_GROUP)[None, None, :, :, None, None]
    m = jnp.maximum(jnp.max(s, axis=-1, keepdims=True), sink)
    e = jnp.exp(s - m)
    denom = jnp.sum(e, axis=-1, keepdims=True) + jnp.exp(sink - m)
    p = (e / denom).astype(v.dtype)
    o = jnp.einsum('bnhgqk,bnkhd->bnqhgd', p, vw)
    return o.reshape(B, S, SWA_WIDTH)

def first_inputs(seed: int = 0) -> dict:
    key = jax.random.key(seed)
    ks = jax.random.split(key, 10)
    x = jax.random.normal(ks[0], (BATCH, SEQ, D_MODEL), jnp.float32)
    norm_g = 1.0 + 0.02 * jax.random.normal(ks[1], (DEPTH, D_MODEL), jnp.float32)
    fox_w_in = jax.random.normal(ks[2], (N_FOX_LAYERS, D_MODEL, FOX_IN), jnp.float32) * D_MODEL ** -0.5
    fox_b_f = (jnp.linspace(1.0, 6.0, FOX_HEADS, dtype=jnp.float32)[None, :]
               + 0.1 * jax.random.normal(ks[3], (N_FOX_LAYERS, FOX_HEADS), jnp.float32))
    fox_w_out = jax.random.normal(ks[4], (N_FOX_LAYERS, FOX_WIDTH, D_MODEL), jnp.float32) * FOX_WIDTH ** -0.5
    swa_w_in = jax.random.normal(ks[5], (N_SWA_LAYERS, D_MODEL, SWA_IN), jnp.float32) * D_MODEL ** -0.5
    swa_sinks = 0.5 * jax.random.normal(ks[6], (N_SWA_LAYERS, SWA_Q_HEADS), jnp.float32)
    swa_w_out = jax.random.normal(ks[7], (N_SWA_LAYERS, SWA_WIDTH, D_MODEL), jnp.float32) * SWA_WIDTH ** -0.5
    final_g = 1.0 + 0.02 * jax.random.normal(ks[8], (D_MODEL,), jnp.float32)
    return {"x": x, "norm_g": norm_g, "fox_w_in": fox_w_in, "fox_b_f": fox_b_f,
            "fox_w_out": fox_w_out, "swa_w_in": swa_w_in, "swa_sinks": swa_sinks,
            "swa_w_out": swa_w_out, "final_g": final_g}

def first_block(x, norm_g, fox_w_in, fox_b_f, fox_w_out, swa_w_in, swa_sinks, swa_w_out, final_g):
    B, S, _ = x.shape
    pos = jnp.arange(S, dtype=jnp.float32)
    for i in range(DEPTH):
        h = rmsnorm(x, norm_g[i])
        j = i // N_MIXERS
        if i % N_MIXERS == 0:
            p = h @ fox_w_in[j]
            W = FOX_WIDTH
            q = p[..., :W].reshape(B, S, FOX_HEADS, FOX_HEAD_DIM)
            k = p[..., W:2 * W].reshape(B, S, FOX_HEADS, FOX_HEAD_DIM)
            v = p[..., 2 * W:3 * W].reshape(B, S, FOX_HEADS, FOX_HEAD_DIM)
            gate = p[..., 3 * W:4 * W]
            log_f = jax.nn.log_sigmoid(p[..., 4 * W:].astype(jnp.float32) + fox_b_f[j].astype(jnp.float32))
            y = fox_attention(q, k, v, log_f)
            w_out = fox_w_out[j]
        else:
            p = h @ swa_w_in[j]
            WQ, WK = SWA_WIDTH, SWA_KV_WIDTH
            q = p[..., :WQ].reshape(B, S, SWA_Q_HEADS, SWA_HEAD_DIM)
            k = p[..., WQ:WQ + WK].reshape(B, S, SWA_KV_HEADS, SWA_HEAD_DIM)
            v = p[..., WQ + WK:WQ + 2 * WK].reshape(B, S, SWA_KV_HEADS, SWA_HEAD_DIM)
            gate = p[..., WQ + 2 * WK:]
            q = partial_rope(q, pos)
            k = partial_rope(k, pos)
            y = swa_attention(q, k, v, swa_sinks[j])
            w_out = swa_w_out[j]
        y = y * jax.nn.silu(gate)
        x = x + y @ w_out
    return rmsnorm(x, final_g)


DEPTH_2 = 1

CHUNK = 64
D_RWKV = D_MODEL // 2
D_HGRN = D_MODEL - D_RWKV
RWKV_HEAD = 64
RWKV_HEADS = D_RWKV // RWKV_HEAD
DECAY_RANK = max(32, int(round(1.8 * D_RWKV ** 0.5 / 32)) * 32)
A_RANK = max(32, int(round(1.8 * D_RWKV ** 0.5 / 32)) * 32)
VRES_RANK = max(32, int(round(1.3 * D_RWKV ** 0.5 / 32)) * 32)
HGRN_EXPAND = 128
HGRN_HEADS = D_HGRN // HGRN_EXPAND
HGRN_HEAD_V = D_HGRN // HGRN_HEADS
RWKV_COLS = 4 * D_RWKV + DECAY_RANK + A_RANK
HGRN_COLS = 4 * D_HGRN
IN_COLS = RWKV_COLS + HGRN_COLS
ALPHA = (2 * DEPTH_2) ** 0.25
BETA = (8 * DEPTH_2) ** -0.25
LN_EPS = 1e-5
GN_EPS = 64e-5
RMS_EPS_2 = 1e-5
LB_FLOOR = 1e-30


def _heads(t, n):
    return t.reshape(t.shape[:-1] + (-1, n))

def _layer_norm(x, w, b):
    x = x.astype(jnp.float32)
    mu = jnp.mean(x, -1, keepdims=True)
    var = jnp.mean(jnp.square(x - mu), -1, keepdims=True)
    return (x - mu) * lax.rsqrt(var + LN_EPS) * w + b

def _token_shift(y, mu):
    y_prev = jnp.pad(y, ((0, 0), (1, 0), (0, 0)))[:, :-1]
    return y + mu * (y_prev - y)

def _rwkv7_scan(r, w, k, v, a_vec, b_vec):
    Bsz, T, H, N = r.shape

    def step(S, inp):
        r_t, w_t, k_t, v_t, a_t, b_t = inp
        sa = jnp.einsum('bhij,bhj->bhi', S, a_t)
        S = S * w_t[:, :, None, :] + sa[..., None] * b_t[:, :, None, :] + v_t[..., None] * k_t[:, :, None, :]
        return S, jnp.einsum('bhij,bhj->bhi', S, r_t)

    S0 = jnp.zeros((Bsz, H, N, N), jnp.float32)
    xs = tuple(jnp.moveaxis(t, 1, 0) for t in (r, w, k, v, a_vec, b_vec))
    _, o = lax.scan(step, S0, xs)
    return jnp.moveaxis(o, 0, 1)

def _rwkv7_branch(rw, v_first, w0, w_up, a0, a_up, k_k, k_a, r_k, gn_w, gn_b, v_mix):
    r, k, v, z, wd, ad = jnp.split(
        rw, [D_RWKV, 2 * D_RWKV, 3 * D_RWKV, 4 * D_RWKV, 4 * D_RWKV + DECAY_RANK], axis=-1)
    w_raw = w0 + jnp.tanh(wd) @ w_up
    decay = jnp.exp(-jnp.exp(-jax.nn.softplus(-w_raw) - 0.5))
    a = jax.nn.sigmoid(a0 + ad @ a_up)
    if v_mix is None:
        v_first = v
    else:
        v0, v_down, v_up = v_mix
        v = v + (v_first - v) * jax.nn.sigmoid(v0 + (v @ v_down) @ v_up)
    kk = _heads(k * k_k, RWKV_HEAD)
    kk = kk / jnp.maximum(jnp.sqrt(jnp.sum(kk * kk, -1, keepdims=True)), 1e-12)
    k = k * (1.0 + (a - 1.0) * k_a)
    rh, kh, vh = _heads(r, RWKV_HEAD), _heads(k, RWKV_HEAD), _heads(v, RWKV_HEAD)
    ah = _heads(a, RWKV_HEAD)
    o = _rwkv7_scan(rh, _heads(decay, RWKV_HEAD), kh, vh, -kk, kk * ah)
    mu = jnp.mean(o, -1, keepdims=True)
    var = jnp.mean(jnp.square(o - mu), -1, keepdims=True)
    o = (o - mu) * lax.rsqrt(var + GN_EPS) * _heads(gn_w, RWKV_HEAD) + _heads(gn_b, RWKV_HEAD)
    o = o + jnp.sum(rh * kh * _heads(r_k, RWKV_HEAD), -1, keepdims=True) * vh
    return o.reshape(rw.shape[:-1] + (D_RWKV,)) * jax.nn.silu(z), v_first

def _hgrn2_chunkwise(q, log_f, k, i):
    Bsz, T, H, DK = q.shape
    DV = i.shape[-1]
    NC = T // CHUNK

    def to_chunks(t):
        return jnp.moveaxis(t.reshape(Bsz, NC, CHUNK, H, t.shape[-1]), 1, 0)

    causal = jnp.tril(jnp.ones((CHUNK, CHUNK), bool))[None, :, :, None, None]

    def step(S, inp):
        q_c, lf_c, k_c, i_c = inp
        b = jnp.cumsum(lf_c, axis=1)
        diff = b[:, :, None] - b[:, None, :]
        decay = jnp.where(causal, jnp.exp(jnp.where(causal, diff, 0.0)), 0.0)
        att = jnp.einsum('btshd,bshd->btsh', q_c[:, :, None] * decay, k_c)
        o_intra = jnp.einsum('btsh,bshv->bthv', att, i_c)
        o_inter = jnp.einsum('bthd,bhdv->bthv', q_c * jnp.exp(b), S)
        b_last = b[:, -1]
        k_dec = k_c * jnp.exp(b_last[:, None] - b)
        S = S * jnp.exp(b_last)[..., None] + jnp.einsum('bshd,bshv->bhdv', k_dec, i_c)
        return S, o_intra + o_inter

    S0 = jnp.zeros((Bsz, H, DK, DV), jnp.float32)
    _, o = lax.scan(step, S0, (to_chunks(q), to_chunks(log_f), to_chunks(k), to_chunks(i)))
    return jnp.moveaxis(o, 0, 1).reshape(Bsz, T, H, DV)

def _hgrn2_branch(hg, lb, g_norm_w):
    q, f_raw, i_in, z = jnp.split(hg, 4, axis=-1)
    q = jax.nn.silu(q)
    log_lb = jnp.log(jnp.maximum(lb, LB_FLOOR))
    log_f = jnp.logaddexp(log_lb, jnp.log1p(-lb) + jax.nn.log_sigmoid(f_raw))
    k = (1.0 - lb) * jax.nn.sigmoid(-f_raw)
    o = _hgrn2_chunkwise(_heads(q, HGRN_EXPAND), _heads(log_f, HGRN_EXPAND),
                         _heads(k, HGRN_EXPAND), _heads(i_in, HGRN_HEAD_V))
    o = o * lax.rsqrt(jnp.mean(o * o, -1, keepdims=True) + RMS_EPS_2)
    return o.reshape(hg.shape[:-1] + (D_HGRN,)) * g_norm_w * jax.nn.silu(z)

def second_inputs(seed: int = 0) -> dict:
    key = jax.random.key(seed)
    ks = jax.random.split(key, 24)
    L, L1 = DEPTH_2, DEPTH_2 - 1

    def nrm(k, shape, s):
        return s * jax.random.normal(k, shape, jnp.float32)

    x = nrm(ks[0], (BATCH, SEQ, D_MODEL), 1.0)
    col_scale = jnp.concatenate([
        jnp.ones((2 * D_RWKV,), jnp.float32), jnp.full((D_RWKV,), BETA, jnp.float32),
        jnp.ones((D_RWKV + DECAY_RANK + A_RANK,), jnp.float32),
        jnp.ones((2 * D_HGRN,), jnp.float32), jnp.full((D_HGRN,), BETA, jnp.float32),
        jnp.ones((D_HGRN,), jnp.float32)])
    w_in = nrm(ks[1], (L, D_MODEL, IN_COLS), D_MODEL ** -0.5) * col_scale
    shift_mu = jax.random.uniform(ks[2], (L, RWKV_COLS), jnp.float32)
    ramp = (jnp.arange(D_RWKV, dtype=jnp.float32) / (D_RWKV - 1)) ** 0.85
    w_decay0 = -6.0 + 5.0 * ramp + nrm(ks[3], (L, D_RWKV), 0.1)
    w_decay_up = nrm(ks[4], (L, DECAY_RANK, D_RWKV), 0.3 * DECAY_RANK ** -0.5)
    a0 = nrm(ks[5], (L, D_RWKV), 0.1)
    a_up = nrm(ks[6], (L, A_RANK, D_RWKV), 0.3 * A_RANK ** -0.5)
    k_k = 0.85 + nrm(ks[7], (L, D_RWKV), 0.05)
    k_a = 1.0 + nrm(ks[8], (L, D_RWKV), 0.05)
    r_k = nrm(ks[9], (L, D_RWKV), 0.1)
    ln_x_w = 1.0 + nrm(ks[10], (L, D_RWKV), 0.05)
    ln_x_b = nrm(ks[11], (L, D_RWKV), 0.02)
    v_mix0 = 1.0 + nrm(ks[12], (L1, D_RWKV), 0.1)
    v_mix_down = nrm(ks[13], (L1, D_RWKV, VRES_RANK), D_RWKV ** -0.5)
    v_mix_up = nrm(ks[14], (L1, VRES_RANK, D_RWKV), 0.3 * VRES_RANK ** -0.5)
    lb_logits = nrm(ks[15], (L, D_HGRN), 0.5)
    g_norm_w = 1.0 + nrm(ks[16], (L, D_HGRN), 0.05)
    w_out = nrm(ks[17], (L, D_MODEL, D_MODEL), BETA * D_MODEL ** -0.5)
    ln_w = 1.0 + nrm(ks[18], (L, D_MODEL), 0.05)
    ln_b = nrm(ks[19], (L, D_MODEL), 0.02)
    return {"x": x, "w_in": w_in, "shift_mu": shift_mu, "w_decay0": w_decay0,
            "w_decay_up": w_decay_up, "a0": a0, "a_up": a_up, "k_k": k_k, "k_a": k_a,
            "r_k": r_k, "ln_x_w": ln_x_w, "ln_x_b": ln_x_b, "v_mix0": v_mix0,
            "v_mix_down": v_mix_down, "v_mix_up": v_mix_up, "lb_logits": lb_logits,
            "g_norm_w": g_norm_w, "w_out": w_out, "ln_w": ln_w, "ln_b": ln_b}

def second_block(x, w_in, shift_mu, w_decay0, w_decay_up, a0, a_up, k_k, k_a, r_k, ln_x_w, ln_x_b,
              v_mix0, v_mix_down, v_mix_up, lb_logits, g_norm_w, w_out, ln_w, ln_b):
    out_dtype = x.dtype
    lb_sm = jax.nn.softmax(lb_logits.astype(jnp.float32), axis=0)
    lower_bounds = jnp.cumsum(lb_sm, axis=0) - lb_sm[0]
    h = x.astype(jnp.float32)
    v_first = None
    for l in range(DEPTH_2):
        proj = jnp.einsum('btd,dc->btc', h, w_in[l].astype(jnp.float32))
        rw = _token_shift(proj[..., :RWKV_COLS], shift_mu[l])
        hg = proj[..., RWKV_COLS:]
        v_mix = None if l == 0 else (v_mix0[l - 1], v_mix_down[l - 1], v_mix_up[l - 1])
        o_rwkv, v_first = _rwkv7_branch(rw, v_first, w_decay0[l], w_decay_up[l], a0[l], a_up[l],
                                        k_k[l], k_a[l], r_k[l], ln_x_w[l], ln_x_b[l], v_mix)
        o_hgrn = _hgrn2_branch(hg, lower_bounds[l], g_norm_w[l])
        y = jnp.einsum('btc,cd->btd', jnp.concatenate([o_rwkv, o_hgrn], axis=-1), w_out[l])
        h = _layer_norm(ALPHA * h + y, ln_w[l], ln_b[l])
    return h.astype(out_dtype)


def setup_inputs(seed=0):
    out = dict(first_inputs(seed))
    for name, value in second_inputs(seed + 1).items():
        if name != "x":
            out[name + "_2"] = value
    return out


def reference(
    x, norm_g, fox_w_in, fox_b_f, fox_w_out, swa_w_in, swa_sinks, swa_w_out, final_g, w_in_2,
    shift_mu_2, w_decay0_2, w_decay_up_2, a0_2, a_up_2, k_k_2, k_a_2, r_k_2, ln_x_w_2, ln_x_b_2,
    v_mix0_2, v_mix_down_2, v_mix_up_2, lb_logits_2, g_norm_w_2, w_out_2, ln_w_2, ln_b_2,
):
    x = first_block(
        x, norm_g, fox_w_in, fox_b_f, fox_w_out, swa_w_in, swa_sinks, swa_w_out, final_g,
    )
    return second_block(
        x, w_in_2, shift_mu_2, w_decay0_2, w_decay_up_2, a0_2, a_up_2, k_k_2, k_a_2, r_k_2,
        ln_x_w_2, ln_x_b_2, v_mix0_2, v_mix_down_2, v_mix_up_2, lb_logits_2, g_norm_w_2,
        w_out_2, ln_w_2, ln_b_2,
    )


_drawn_inputs = setup_inputs


def setup_inputs(seed=0):
    import zlib

    import numpy as np

    out = dict(_drawn_inputs(seed))
    spreads = {}
    factors = {'norm_g': 6.604,
     'swa_sinks': 34.329,
     'final_g': 2.683,
     'w_decay_up_2': 8.0,
     'a0_2': 7.577,
     'a_up_2': 2.82,
     'k_k_2': 45.332,
     'k_a_2': 6.186,
     'ln_x_w_2': 20.57,
     'ln_x_b_2': 47.664,
     'g_norm_w_2': 15.595,
     'ln_b_2': 2.809}
    for name, (base, spread) in spreads.items():
        noise = np.random.default_rng([zlib.crc32(name.encode()), seed]).standard_normal(out[name].shape)
        drawn = base * np.exp(spread * noise) if base else spread * noise
        out[name] = __import__('jax').numpy.asarray(drawn.astype(out[name].dtype))
    for name, factor in factors.items():
        out[name] = (out[name] * factor).astype(out[name].dtype)
    return out
```

```python
from contextlib import ExitStack

import numpy as np

import concourse.bass as bass
from concourse import mybir

F32 = mybir.dt.float32
F32R = mybir.dt.float32r
BF16 = mybir.dt.bfloat16
U8 = mybir.dt.uint8
ALU = mybir.AluOpType
ACT = mybir.ActivationFunctionType
AX_X = mybir.AxisListType.X

P = 128
D = 2048
SEQ = 512
TT = SEQ // P
KT = D // P
N = 512
HD = 64
GROUPS = D // N
GH = N // HD
FOX_HEADS = D // HD
SLOTS = 8
RW = 1024
CH = 128
NCH = SEQ // CH
LEVELS = 7
HALF = 256
RANK = 64
ROT = 8
ALPHA = 2.0 ** 0.25
NEG = -1e30
RMS_EPS = 1e-6
LN_EPS = 1e-5
GN_EPS = 64e-5
HGRN_EPS = 1e-5
LB_FLOOR = 1e-30
LB_SCALE = 2.0 ** 90
EXP_HALF = float(np.exp(-0.5))
FOX_SLOTS, OUT_SLOTS, SWA_SLOTS, BR_SLOTS = 4 * 4 * 4, 4 * 4, 4 * 2 * 4, 4 * 8
ALL_SLOTS = FOX_SLOTS + OUT_SLOTS + SWA_SLOTS + OUT_SLOTS + 2 * BR_SLOTS + OUT_SLOTS


def at(i, rate, k):
    return k if i is None else i * rate + k


def build(nc, a, out):
    with ExitStack() as ctx:
        def sb(name, shape, dt=F32):
            return ctx.enter_context(nc.sbuf_tensor(name, shape, dt))

        def sem(name):
            return ctx.enter_context(nc.semaphore(name))

        def twin(name, shape):
            with nc.sbuf_tensor(name, shape, F32) as plain:
                pass
            return plain, sb(name + "_split", shape, F32R)

        r1, r1_split = twin("r1", [P, KT * SEQ])
        r2, r2_split = twin("r2", [P, KT * SEQ])
        wring, wring_split = twin("wring", [P, SLOTS, 4 * N])
        ws, ws_split = twin("ws", [P, 20900])
        banks = [ctx.enter_context(nc.psum_tensor(f"bank{b}", [P, N], F32)) for b in range(8)]
        ident = sb("ident", [P, P])
        identb = sb("identb", [P, P], BF16)
        maskb = sb("maskb", [P, 2 * P], BF16)
        tril4 = sb("tril4", [P, 4 * P], U8)
        lmask = sb("lmask", [P, LEVELS, P], U8)
        lmaskt = sb("lmaskt", [P, LEVELS + 1, P], U8)
        small = sb("small", [P, 256])

        def tok(r):
            return r[:].rearrange("p (t n) -> p t n", t=TT)

        def chan(r):
            return r[:].rearrange("p (k s) -> p k s", k=KT)

        class Carve:
            def __init__(self, region, at_=0):
                self.region, self.at = region, at_

            def __call__(self, *shape, dt=F32):
                n = int(np.prod(shape))
                words = n if dt == F32 else (n * 2 + 3) // 4
                v = self.region[:, self.at:self.at + words]
                self.at += words
                assert self.at <= self.region.shape[1], self.at
                if dt != F32:
                    v = v.bitcast(dt)
                names = "abcd"[:len(shape)]
                if len(shape) > 1:
                    v = v.rearrange(f"p ({' '.join(names)}) -> p {' '.join(names)}",
                                    **{x: s for x, s in zip(names, shape)})
                return v

        consts_in = sem("consts_in")
        w_full = [sem(f"w_full{s}") for s in range(SLOTS)]
        w_free = sem("w_free")
        gemm_done = sem("gemm_done")
        taken = [sem("taken0"), sem("taken1")]
        tr_done = sem("tr_done")
        tr_out = [sem("tr_out_act"), sem("tr_out_dve")]
        phase_end = {e: sem(f"phase_end_{e}") for e in ("pe", "act", "dve", "pool")}
        dve_step, act_step, pool_step = sem("dve_step"), sem("act_step"), sem("pool_step")

        class Tally:
            def __init__(self):
                self.jobs = self.uses = self.turns = self.slots = 0
        PE_T, ACT_T, DVE_T = Tally(), Tally(), Tally()
        phases = {"pe": 0, "act": 0, "dve": 0, "pool": 0}

        def barrier(name, eng):
            phases[name] += 1
            eng.drain().then_inc(phase_end[name], 1)
            for other, s in phase_end.items():
                if other != name:
                    eng.wait_ge(s, phases[name])

        class Steps:
            def __init__(self, eng, s):
                self.eng, self.s, self.base, self.n, self.i, self.rate = eng, s, 0, 0, None, 0

            def __call__(self, ins):
                self.n += 1
                ins.then_inc(self.s, 1)
                self.eng.wait_ge(self.s, at(self.i, self.rate, self.base + self.n))

            def enter(self, i, rate):
                self.base += self.n
                self.n, self.i, self.rate = 0, i, rate

            def leave(self, rounds):
                assert self.n == self.rate, f"steps per round: {self.n}, not {self.rate}"
                self.base, self.n, self.i = self.base + rounds * self.rate, 0, None

        class Gemm:
            def __init__(self, tally, i=None, jrate=0, urate=0):
                self.t, self.i, self.jr, self.ur, self.u = tally, i, jrate, urate, 0

            def claim(self, eng):
                n = self.t.uses + self.u
                self.u += 1
                eng.wait_ge(taken[n % 2], 1 + at(self.i, self.ur // 2, n // 2))
                return banks[n % 2]

            def bank(self, u):
                n = self.t.uses + u
                return banks[n % 2], taken[n % 2]

            def product(self, eng, j):
                eng.wait_ge(gemm_done, at(self.i, self.jr, self.t.jobs + j + 1))
                return self.bank(j)

            def wait_taken(self, eng, u):
                n = self.t.uses + u
                eng.wait_ge(taken[n % 2], 1 + at(self.i, self.ur // 2, n // 2 + 1))

            def close(self, rounds, jobs, uses):
                self.t.jobs += jobs * rounds
                self.t.uses += uses * rounds

        class Turns:
            def __init__(self, tally, i=None, rate=0):
                self.t, self.i, self.rate, self.n = tally, i, rate, 0

            def claim(self, eng):
                n = self.n
                self.n += 1
                eng.wait_ge(tr_out[n % 2], at(self.i, self.rate // 2, self.t.turns // 2 + n // 2))
                return banks[6 + n % 2]

            def wait(self, eng, n):
                eng.wait_ge(tr_done, at(self.i, self.rate, self.t.turns + n + 1))
                return banks[6 + n % 2], tr_out[n % 2]

            def wait_out(self, eng, n):
                eng.wait_ge(tr_out[n % 2], at(self.i, self.rate // 2, self.t.turns // 2 + n // 2 + 1))

            def close(self, n, rounds=1):
                self.t.turns += n * rounds
                assert n % 2 == 0

        class Slots:
            def __init__(self, i=None, rate=0):
                self.i, self.rate, self.n = i, rate, 0

            def wait(self, pe, s):
                k = PE_T.slots + s
                pe.wait_ge(w_full[k % SLOTS], at(self.i, 16 * self.rate // SLOTS, 16 * (k // SLOTS + 1)))
                return wring[:, k % SLOTS, :]

            def close(self, rounds=1):
                PE_T.slots += self.n * rounds

        def weights_steps(pe, g, sl, act_t, width, by_channel):
            per = 4 * N // width
            jobs = width // P if by_channel else TT
            first = sl.n
            sl.n += KT // per
            for j in range(jobs):
                bank = g.claim(pe)
                for kt in range(KT):
                    if kt % per == 0:
                        w = sl.wait(pe, first + kt // per).rearrange("p (k n) -> p k n", n=width)
                    if by_channel:
                        mm = pe.matmul(bank[:], w[:, kt % per, j * P:(j + 1) * P], act_t[:, kt, :],
                                       start=(kt == 0), stop=(kt == KT - 1))
                    else:
                        mm = pe.matmul(bank[:, 0:width], act_t[:, kt, j * P:(j + 1) * P], w[:, kt % per, :],
                                       start=(kt == 0), stop=(kt == KT - 1))
                    if (j == 0 and kt == 0) or (j == jobs - 1 and kt % per == per - 1 and kt < KT - 1):
                        mm.then_inc(w_free, 1)
                    if kt == KT - 1:
                        mm.then_inc(gemm_done, 1)
                    yield True

        def weights(*args, **how):
            for _ in weights_steps(*args, **how):
                pass

        def small_weights(pe, g, w, act_t, width, by_channel):
            for j in range(1 if by_channel else TT):
                bank = g.claim(pe)
                for kt in range(KT):
                    if by_channel:
                        mm = pe.matmul(bank[0:width, :], w[:, kt, :], act_t[:, kt, :],
                                       start=(kt == 0), stop=(kt == KT - 1))
                    else:
                        mm = pe.matmul(bank[:, 0:width], act_t[:, kt, j * P:(j + 1) * P], w[:, kt, :],
                                       start=(kt == 0), stop=(kt == KT - 1))
                mm.then_inc(gemm_done, 1)

        x_in = [sem(f"x_in{t}") for t in range(TT)]
        g_in = sem("g_in")
        norm_root, xn_ready, stored = sem("norm_root"), sem("xn_ready"), sem("stored")
        nm = Carve(ws)
        n_gain, n_xn, n_junk = nm(D), nm(TT, D), nm(D)
        MASKS = 4 + LEVELS + LEVELS + 1
        masks = ws[:, nm.at:nm.at + MASKS * P].bitcast(mybir.dt.int32)
        ss, root, rstd = small[:, 0:4], small[:, 4:8], small[:, 8:12]
        eps = {e: small[:, 12 + k:13 + k] for k, e in enumerate((RMS_EPS, LN_EPS, GN_EPS, HGRN_EPS))}

        def norm_pool(pool, n, src):
            pool.dma_start(n_gain, a["gains"][n:n + 1, :].broadcast_to([P, D])).then_inc(g_in, 16)
            if n == 0:
                for t in range(TT):
                    pool.dma_start(tok(src)[:, t, :], a["x"][t * P:(t + 1) * P, :]).then_inc(x_in[t], 16)
            if n == 1:
                pool.dma_start(a["x1"].rearrange("(t p) n -> p t n", p=P), tok(src)).then_inc(stored, 16)
                pool.wait_ge(stored, 16)
            if n == 2:
                for t in range(TT):
                    pool.wait_ge(xn_ready, 4 * n + t + 1)
                    pool.dma_start(a["x2"][t * P:(t + 1) * P, :], n_xn[:, t, :]).then_inc(stored, 16)
                pool.wait_ge(stored, 16 * (1 + TT))

        def norm_act(act, st, n, src, dst):
            for t in range(TT):
                if n == 0:
                    act.wait_ge(x_in[t], 16)
                st(act.activation(n_junk, tok(src)[:, t, :], ACT.Square, accum_out=ss[:, t:t + 1]))
            act.activation(root, ss, ACT.Sqrt, bias=eps[RMS_EPS], scale=1.0 / D).then_inc(norm_root, 1)
            norm_out(act, n, dst, 0, ACT_T)

        def norm_dve(dve, st, n, src, dst):
            dve.wait_ge(norm_root, n + 1)
            st(dve.reciprocal(rstd, root))
            dve.wait_ge(g_in, 16 * (n + 1))
            tr = Turns(DVE_T)
            for t in range(TT):
                dve.scalar_tensor_tensor(n_xn[:, t, :], tok(src)[:, t, :], rstd[:, t:t + 1], n_gain,
                                         ALU.mult, ALU.mult).then_inc(xn_ready, 1)
                norm_out_t(dve, tr, t, dst, 1)
            tr.close(4 * TT)

        def norm_out_t(eng, tr, t, dst, par):
            for q in range(4):
                turn = 4 * t + q
                if turn % 2 == par:
                    bank, out_sem = tr.wait(eng, turn)
                    to = chan(dst)[:, 4 * q:4 * q + 4, t * P:(t + 1) * P]
                    frm = bank[:].rearrange("p (k s) -> p k s", k=4)
                    (eng.activation(to, frm, ACT.Copy) if par == 0 else eng.tensor_copy(to, frm)).then_inc(out_sem, 1)

        def norm_out(eng, n, dst, par, tally):
            tr = Turns(tally)
            for t in range(TT):
                norm_out_t(eng, tr, t, dst, par)
            tr.close(4 * TT)

        def norm_pe(pe, n):
            tr = Turns(PE_T)
            for t in range(TT):
                pe.wait_ge(xn_ready, 4 * n + t + 1)
                for q in range(4):
                    bank = tr.claim(pe)
                    for k in range(4):
                        mm = pe.transpose(bank[:, k * P:(k + 1) * P],
                                          n_xn[:, t, (4 * q + k) * P:(4 * q + k + 1) * P], ident[:])
                    mm.then_inc(tr_done, 1)
            tr.close(4 * TT)

        res_in = sem("res_in")
        res = Carve(ws)(GROUPS, TT, N)

        def outp_pool(pool, n):
            frm = (a["x"], a["x1"], a["x2"])[n]
            for g in range(GROUPS):
                pool.dma_start(res[:, g, :, :], frm.rearrange("(t p) n -> p t n", p=P)[:, :, g * N:(g + 1) * N]
                               ).then_inc(res_in, 16)

        y_hi_ready, y_lo_ready = sem("y_high_ready"), sem("y_low_ready")
        w_hi_ready, w_lo_ready = sem("w_high_ready"), sem("w_low_ready")
        out_taken = sem("out_taken")
        HI_SLOTS = 2
        y_hi = ws_split[:, 8192:16384].rearrange("p (k s) -> p k s", k=KT)
        w_hi = ws_split[:, 16384:16384 + HI_SLOTS * 4 * N].rearrange("p (s w) -> p s w", s=HI_SLOTS)
        OUT_AT = (FOX_SLOTS, FOX_SLOTS + OUT_SLOTS + SWA_SLOTS, ALL_SLOTS - OUT_SLOTS)

        def outp_pe(pe, n, y_lo):
            assert PE_T.slots == OUT_AT[n]
            y_lo = chan(y_lo)
            with pe.Fori(0, GROUPS // 2) as i:
                for k in range(2):
                    for kt in range(KT):
                        s = 4 * k + kt // 4
                        c = slice(kt % 4 * N, kt % 4 * N + N)
                        if kt % 4 == 0:
                            if k == 0:
                                pe.wait_ge(y_hi_ready, 4 * n + kt // 4 + 1)
                                pe.wait_ge(y_lo_ready, 4 * n + kt // 4 + 1)
                            pe.wait_ge(w_hi_ready, at(i, 8, OUT_SLOTS * n + s + 1))
                            pe.wait_ge(w_lo_ready, at(i, 8, OUT_SLOTS * n + s + 1))
                        for t in range(TT):
                            job = TT * k + t
                            if kt == 0:
                                pe.wait_ge(out_taken, at(i, 8, 16 * n + job + 1))
                            hi = y_hi[:, kt, t * P:(t + 1) * P]
                            mm = pe.matmul(banks[job][:], hi, w_hi[:, s % HI_SLOTS, c], start=(kt == 0), stop=False)
                            if kt == 0 and t == 0:
                                mm.then_inc(w_free, 1)
                            pe.matmul(banks[job][:], hi, wring_split[:, s, c], start=False, stop=False)
                            mm = pe.matmul(banks[job][:], y_lo[:, kt, t * P:(t + 1) * P], w_hi[:, s % HI_SLOTS, c],
                                           start=False, stop=(kt == KT - 1))
                            if kt == KT - 1:
                                mm.then_inc(gemm_done, 1)
                            elif kt % 4 == 3 and t == TT - 1:
                                mm.then_inc(w_free, 1)
            PE_T.jobs += 16
            PE_T.slots += OUT_SLOTS

        def outp_act(act, n, y):
            for c in range(4):
                act.activation(y_hi[:, 4 * c:4 * c + 4, :], chan(y)[:, 4 * c:4 * c + 4, :], ACT.Copy
                               ).then_inc(y_hi_ready, 1)
            with act.Fori(0, GROUPS // 2) as i:
                for s in range(8):
                    act.wait_ge(w_full[s], at(i, 16, OUT_AT[n] // SLOTS * 16 + 16))
                    act.wait_ge(w_free, at(i, 8, OUT_AT[n] + s))
                    act.activation(w_hi[:, s % HI_SLOTS, :], wring[:, s, :], ACT.Copy).then_inc(w_hi_ready, 1)
            ACT_T.jobs += 16

        def outp_dve(dve, n, y, y_lo, dst):
            for c in range(4):
                dve.wait_ge(y_hi_ready, 4 * n + c + 1)
                dve.tensor_tensor(chan(y_lo)[:, 4 * c:4 * c + 4, :], chan(y)[:, 4 * c:4 * c + 4, :],
                                  y_hi[:, 4 * c:4 * c + 4, :].bitcast(F32), ALU.subtract).then_inc(y_lo_ready, 1)

            def low(s):
                dve.wait_ge(w_hi_ready, OUT_SLOTS * n + s + 1)
                dve.tensor_tensor(wring_split[:, s % SLOTS, :], wring[:, s % SLOTS, :],
                                  w_hi[:, s % HI_SLOTS, :].bitcast(F32), ALU.subtract).then_inc(w_lo_ready, 1)

            low(0)
            for g in range(GROUPS):
                for s in range(4 * g + 1, min(4 * g + 5, OUT_SLOTS)):
                    low(s)
                if g == 0:
                    dve.wait_ge(res_in, 16 * GROUPS * (n + 1))
                for t in range(TT):
                    job = TT * g + t
                    dve.wait_ge(gemm_done, DVE_T.jobs + job + 1)
                    dve.scalar_tensor_tensor(tok(dst)[:, t, g * N:(g + 1) * N], res[:, g, t, :],
                                             ALPHA if n == 2 else 1.0, banks[job % 8][:],
                                             ALU.mult, ALU.add).then_inc(out_taken, 1)
            DVE_T.jobs += 16

        wx_in = sem("wx_in")
        fg_ready, c_stored, c3_in = sem("fg_ready"), sem("c_stored"), sem("c3_in")
        fa, fexp = sem("fa"), sem("fexp")
        fc = Carve(ws)
        f_w, f_b = fc(KT, FOX_HEADS), fc(1)
        f_x, f_a, f_e, f_l, f_m, f_c, f_one = fc(N), fc(N), fc(N), fc(N), fc(N), fc(N), fc(N)
        f_3 = [fc(N, dt=BF16) for _ in range(3)]

        def forget_pool(pool):
            pool.dma_start(f_w, a["w_f"]).then_inc(wx_in, 16)
            pool.dma_start(f_b[0:FOX_HEADS, :], a["b_f"]).then_inc(wx_in, 16)
            pool.wait_ge(fg_ready, 3)
            for k in range(3):
                pool.dma_start(a["c3"][k:k + 1, :].rearrange("o (h s) -> (o h) s", h=FOX_HEADS),
                               f_3[k][0:FOX_HEADS, :]).then_inc(c_stored, 16)
            pool.wait_ge(c_stored, 48)

        def forget_pe(pe, ht):
            pe.wait_ge(wx_in, 32)
            g = Gemm(PE_T)
            small_weights(pe, g, f_w, chan(ht), FOX_HEADS, by_channel=True)
            g.close(1, 1, 1)

        def forget_dve(dve, st):
            h = slice(0, FOX_HEADS)
            st(dve.memset(f_one[h, :], 1.0))
            g = Gemm(DVE_T)
            bank, out_sem = g.product(dve, 0)
            dve.wait_ge(wx_in, 32)
            dve.tensor_scalar(f_x[h, :], bank[h, :], f_b[h, 0:1], None, ALU.add).then_inc(out_sem, 1)
            g.wait_taken(dve, 0)
            g.close(1, 1, 1)
            st(dve.tensor_scalar(f_a[h, :], f_x[h, :], -1.0, None, ALU.mult))
            dve.tensor_tensor(f_a[h, :], f_a[h, :], f_x[h, :], ALU.max).then_inc(fa, 1)
            dve.wait_ge(fexp, 2)
            st(dve.tensor_scalar(f_m[h, :], f_x[h, :], 0.0, None, ALU.min))
            st(dve.tensor_tensor(f_m[h, :], f_m[h, :], f_l[h, :], ALU.subtract))
            st(dve.tensor_tensor_scan(f_c[h, :], f_one[h, :], f_m[h, :], 0.0, ALU.mult, ALU.add))
            st(dve.tensor_scalar(f_c[h, :], f_c[h, :], -1.0, None, ALU.mult))
            for k in range(3):
                dve.tensor_copy(f_3[k][h, :], f_c[h, :]).then_inc(fg_ready, 1)
                if k < 2:
                    dve.wait_ge(fg_ready, k + 1)
                    st(dve.tensor_tensor(f_c[h, :], f_c[h, :], f_3[k][h, :], ALU.subtract))

        def forget_act(act):
            h = slice(0, FOX_HEADS)
            act.wait_ge(fa, 1)
            act.activation(f_e[h, :], f_a[h, :], ACT.Exp, scale=-1.0).then_inc(fexp, 1)
            act.wait_ge(fexp, 1)
            act.activation(f_l[h, :], f_e[h, :], ACT.Ln, bias=1.0).then_inc(fexp, 1)

        UNITS = GH * TT
        s_done = {m: sem(f"scores_done_{m}") for m in ("fox", "swa")}
        max_ready = {m: sem(f"max_ready_{m}") for m in ("fox", "swa")}
        probs = {m: sem(f"probs_ready_{m}") for m in ("fox", "swa")}
        av_done = {m: sem(f"av_done_{m}") for m in ("fox", "swa")}
        y_ready = {m: sem(f"y_ready_{m}") for m in ("fox", "swa")}
        q_in, k_in = sem("q_turned_by_position"), sem("k_turned_by_position")
        sig_in = {m: sem(f"gate_sigmoid_{m}") for m in ("fox", "swa")}
        sinks_exp = sem("sinks_exp")
        ac = Carve(ws)
        qz, gate, yt = ac(4, 2, N), ac(TT, N), ac(TT, N)
        prob, probt = ac(3, N), ac(2, N)
        nmax, rsum, den, rden = ac(UNITS), ac(UNITS), ac(UNITS), ac(UNITS)
        both = ac.at
        kt_, vt, c3g, ones3 = ac(4, N), ac(TT, N), ac(GH, N, dt=BF16), ac(P, dt=BF16)
        ac.at = both
        w_kv, qtok, kvtok, kdup, kt2 = ac(KT, P), ac(TT, N), ac(TT, P), ac(TT, P), ac(N)
        cos_, sin_ = ac(TT, ROT), ac(TT, ROT)
        ra, rb_, rc, rd = [ac(TT * GH * ROT) for _ in range(4)]
        sinkb, sk8, nsk8, nmax2, esink = ac(FOX_HEADS), ac(GH), ac(GH), ac(UNITS), ac(UNITS)

        def keys(m, b):
            return (0, (b + 1) * P) if m == "fox" else (max(b - 1, 0) * P, min(b + 1, 2) * P)

        wkv_in, rope_in, sink_in = sem("wkv_in"), sem("rope_in"), sem("sink_in")
        JR = {"fox": (16, 24), "swa": (12, 20)}
        T0 = {"fox": 0, "swa": 6}
        TR = {"fox": UNITS + 4, "swa": UNITS + 10}

        def attn_pe(pe, m, ht):
            with pe.Fori(0, GROUPS) as i:
                g, tr, sl = Gemm(PE_T, i, *JR[m]), Turns(PE_T, i, TR[m]), Slots(i, 16 if m == "fox" else 8)
                if m == "fox":
                    weights(pe, g, sl, chan(ht), N, by_channel=True)
                    weights(pe, g, sl, chan(ht), N, by_channel=True)
                    weights(pe, g, sl, chan(ht), N, by_channel=False)
                    weights(pe, g, sl, chan(ht), N, by_channel=False)
                    for j in (10, 11):
                        g.wait_taken(pe, j)
                    pe.wait_ge(c3_in, i * 16 + 16)
                else:
                    pe.wait_ge(wkv_in, i * 16 + 16)
                    small_weights(pe, g, w_kv, chan(ht), P, by_channel=False)
                    weights(pe, g, sl, chan(ht), N, by_channel=False)
                    weights(pe, g, sl, chan(ht), N, by_channel=False)
                    pe.wait_ge(k_in, i + 1)
                    for half in range(2):
                        bank = tr.claim(pe)
                        for t in range(2):
                            mm = pe.transpose(bank[:, t * P:(t + 1) * P], kdup[:, 2 * half + t, :], ident[:])
                        mm.then_inc(tr_done, 1)
                    pe.wait_ge(q_in, i + 1)
                    for ct in range(4):
                        bank = tr.claim(pe)
                        for t in range(TT):
                            mm = pe.transpose(bank[:, t * P:(t + 1) * P], qtok[:, t, ct * P:(ct + 1) * P], ident[:])
                        mm.then_inc(tr_done, 1)
                    for n in (4, 5):
                        tr.wait_out(pe, n)

                def scores(u):
                    h, b = divmod(u, TT)
                    k0, nk = keys(m, b)
                    bank = banks[2 + u % 4]
                    pe.wait_ge(probs[m], 1 + i * UNITS + max(0, u - 3))
                    kv = kt_[:, h // 2, k0:k0 + nk] if m == "fox" else kt2[:, k0:k0 + nk]
                    pe.matmul(bank[:, 0:nk], qz[:, h // 2, h % 2, b * P:(b + 1) * P], kv, start=True, stop=False)
                    if m == "fox":
                        pe.matmul(bank[:, 0:nk], ones3, c3g[:, h, 0:nk], start=False, stop=False)
                    wide = P if m == "fox" or b == 0 else 2 * P
                    pe.matmul(bank[:, nk - wide:nk], identb[:], maskb[:, 2 * P - wide:2 * P],
                              start=False, stop=True).then_inc(s_done[m], 1)

                def turn(u):
                    pe.wait_ge(probs[m], 1 + i * UNITS + u + 1)
                    bank = tr.claim(pe)
                    for kb in range(keys(m, u % TT)[1] // P):
                        mm = pe.transpose(bank[:, kb * P:(kb + 1) * P], prob[:, u % 3, kb * P:(kb + 1) * P], ident[:])
                    mm.then_inc(tr_done, 1)

                obank = {}

                def values(u):
                    h, b = divmod(u, TT)
                    k0, nk = keys(m, b)
                    if b == 0:
                        obank[h] = g.claim(pe)
                    tr.wait_out(pe, T0[m] + u)
                    for kb in range(nk // P):
                        v = vt[:, k0 // P + kb, h * HD:(h + 1) * HD] if m == "fox" else kvtok[:, k0 // P + kb, HD:2 * HD]
                        mm = pe.matmul(obank[h][:, b * HD:(b + 1) * HD], probt[:, u % 2, kb * P:(kb + 1) * P], v,
                                       start=(kb == 0), stop=(kb == nk // P - 1))
                    mm.then_inc(av_done[m], 1)

                for n in range(UNITS + 3):
                    if n < UNITS:
                        scores(n)
                    if 2 <= n < UNITS + 2:
                        turn(n - 2)
                    if n >= 3:
                        values(n - 3)
                pe.wait_ge(y_ready[m], 1 + i + 1)
                for t in range(TT):
                    bank = tr.claim(pe)
                    for ct in range(4):
                        mm = pe.transpose(bank[:, ct * P:(ct + 1) * P], yt[:, t, ct * P:(ct + 1) * P], ident[:])
                    mm.then_inc(tr_done, 1)
                assert g.u == JR[m][1] and tr.n == TR[m]
            g.close(GROUPS, *JR[m]), sl.close(GROUPS), tr.close(TR[m], GROUPS)

        def attn_turn_out(eng, i, m, tr, u):
            if u % 2 == (eng is nc.vector):
                bank, out_sem = tr.wait(eng, T0[m] + u)
                eng.wait_ge(av_done[m], 1 + i * UNITS + max(0, u - 1))
                nk = keys(m, u % TT)[1]
                if eng is nc.vector:
                    eng.tensor_copy(probt[:, u % 2, 0:nk], bank[:, 0:nk]).then_inc(out_sem, 1)
                else:
                    eng.activation(probt[:, u % 2, 0:nk], bank[:, 0:nk], ACT.Copy).then_inc(out_sem, 1)

        def y_out(eng, i, m, tr, dst):
            for t in range(TT):
                if t % 2 == (eng is nc.vector):
                    bank, out_sem = tr.wait(eng, T0[m] + UNITS + t)
                    to = chan(dst)[:, bass.ds(i * 4, 4), t * P:(t + 1) * P]
                    frm = bank[:].rearrange("p (k s) -> p k s", k=4)
                    (eng.tensor_copy(to, frm) if eng is nc.vector else
                     eng.activation(to, frm, ACT.Copy)).then_inc(out_sem, 1)

        def attn_act(act, st, m, dst):
            with act.Fori(0, GROUPS) as i:
                g, tr = Gemm(ACT_T, i, *JR[m]), Turns(ACT_T, i, TR[m])
                st.enter(i, {"fox": 4, "swa": 2}[m])
                if m == "fox":
                    for ct in range(4):
                        bank, out_sem = g.product(act, ct)
                        st(act.activation(qz[0:HD, ct, 0, :], bank[0:HD, :], ACT.Copy, scale=0.125))
                        act.activation(qz[HD:P, ct, 1, :], bank[HD:P, :], ACT.Copy, scale=0.125).then_inc(out_sem, 1)
                    for t in range(TT):
                        bank, out_sem = g.product(act, 8 + t)
                        act.activation(vt[:, t, :], bank[:], ACT.Copy).then_inc(out_sem, 1)
                else:
                    for t in range(TT):
                        bank, out_sem = g.product(act, t)
                        act.activation(kvtok[:, t, :], bank[:, 0:P], ACT.Copy).then_inc(out_sem, 1)
                    for t in range(TT):
                        bank, out_sem = g.product(act, 4 + t)
                        act.activation(qtok[:, t, :], bank[:], ACT.Copy, scale=0.125).then_inc(out_sem, 1)
                act.wait_ge(y_ready[m], 1 + i)
                for t in range(TT):
                    bank, _ = g.product(act, JR[m][0] - 4 + t)
                    act.activation(gate[:, t, :], bank[:], ACT.Sigmoid).then_inc(sig_in[m], 1)
                if m == "swa":
                    bank, out_sem = tr.wait(act, 0)
                    act.activation(kt2[:, 0:2 * P], bank[:, 0:2 * P], ACT.Copy).then_inc(out_sem, 1)
                    for ct in (0, 2):
                        bank, out_sem = tr.wait(act, 2 + ct)
                        st(act.activation(qz[0:HD, ct, 0, :], bank[0:HD, :], ACT.Copy))
                        act.activation(qz[HD:P, ct, 1, :], bank[HD:P, :], ACT.Copy).then_inc(out_sem, 1)
                for n in range(UNITS + 2):
                    if n < UNITS:
                        h, b = divmod(n, TT)
                        nk = keys(m, b)[1]
                        act.wait_ge(max_ready[m], i * UNITS + n + 1)
                        act.wait_ge(tr_done, at(i, TR[m], ACT_T.turns + (T0[m] + n - 2 if n >= 3 else 0)))
                        act.activation(prob[:, n % 3, 0:nk], banks[2 + n % 4][:, 0:nk], ACT.Exp,
                                       bias=(nmax if m == "fox" else nmax2)[:, n:n + 1],
                                       accum_out=rsum[:, n:n + 1]).then_inc(probs[m], 1)
                        if m == "swa" and b == TT - 1:
                            act.activation(esink[:, 4 * h:4 * h + 4], nmax2[:, 4 * h:4 * h + 4], ACT.Exp,
                                           bias=sk8[:, h:h + 1]).then_inc(sinks_exp, 1)
                    if n >= 2:
                        attn_turn_out(act, i, m, tr, n - 2)
                y_out(act, i, m, tr, dst)
            st.leave(GROUPS)
            g.close(GROUPS, *JR[m]), tr.close(TR[m], GROUPS)

        def attn_dve(dve, st, m, dst):
            st(dve.memset(qz[0:HD, :, 1, :], 0.0))
            st(dve.memset(qz[HD:P, :, 0, :], 0.0))
            if m == "swa":
                dve.wait_ge(rope_in, 48)
            with dve.Fori(0, GROUPS) as i:
                g, tr = Gemm(DVE_T, i, *JR[m]), Turns(DVE_T, i, TR[m])
                st.enter(i, {"fox": 8, "swa": 63}[m])
                if m == "fox":
                    for ct in range(4):
                        bank, out_sem = g.product(dve, 4 + ct)
                        dve.tensor_copy(kt_[:, ct, :], bank[:]).then_inc(out_sem, 1)
                else:
                    st(dve.tensor_copy(sk8, sinkb[:, bass.ds(i * GH, GH)]))
                    st(dve.tensor_scalar(nsk8, sk8, -1.0, None, ALU.mult))

                    def rope(x, heads):
                        x1, x2 = x[:, :, :, 0:ROT], x[:, :, :, ROT:2 * ROT]
                        cs = cos_.unsqueeze(2).broadcast_to([P, TT, heads, ROT])
                        sn = sin_.unsqueeze(2).broadcast_to([P, TT, heads, ROT])
                        v = [r[:, 0:TT * heads * ROT].rearrange("p (t h r) -> p t h r", t=TT, h=heads)
                             for r in (ra, rb_, rc, rd)]
                        st(dve.tensor_tensor(v[0], x1, cs, ALU.mult))
                        st(dve.tensor_tensor(v[1], x2, sn, ALU.mult))
                        st(dve.tensor_tensor(v[2], x2, cs, ALU.mult))
                        st(dve.tensor_tensor(v[3], x1, sn, ALU.mult))
                        st(dve.tensor_tensor(x1, v[0], v[1], ALU.subtract))
                        return dve.tensor_tensor(x2, v[2], v[3], ALU.add)

                    for j in (2, 3):
                        g.wait_taken(dve, j)
                    st(rope(kvtok.rearrange("p t (h d) -> p t h d", h=2)[:, :, 0:1, :], 1))
                    dve.tensor_copy(kdup.rearrange("p t (h d) -> p t h d", h=2),
                                    kvtok[:, :, 0:HD].unsqueeze(2).broadcast_to([P, TT, 2, HD])).then_inc(k_in, 1)
                    for j in (6, 7):
                        g.wait_taken(dve, j)
                    rope(qtok.rearrange("p t (h d) -> p t h d", h=GH), GH).then_inc(q_in, 1)
                for t in range(TT):
                    bank, out_sem = g.product(dve, JR[m][0] - 4 + t)
                    dve.wait_ge(sig_in[m], i * 4 + t + 1)
                    dve.tensor_tensor(gate[:, t, :], bank[:], gate[:, t, :], ALU.mult).then_inc(out_sem, 1)
                if m == "swa":
                    bank, out_sem = tr.wait(dve, 1)
                    dve.tensor_copy(kt2[:, 2 * P:4 * P], bank[:, 0:2 * P]).then_inc(out_sem, 1)
                    for ct in (1, 3):
                        bank, out_sem = tr.wait(dve, 2 + ct)
                        st(dve.tensor_copy(qz[0:HD, ct, 0, :], bank[0:HD, :]))
                        dve.tensor_copy(qz[HD:P, ct, 1, :], bank[HD:P, :]).then_inc(out_sem, 1)

                def head_out(h):
                    dve.wait_ge(av_done[m], 1 + i * UNITS + 4 * h + 4)
                    dve.wait_ge(probs[m], 1 + i * UNITS + 4 * h + 4)
                    c = slice(4 * h, 4 * h + 4)
                    if m == "swa":
                        dve.wait_ge(sinks_exp, i * GH + h + 1)
                        st(dve.tensor_tensor(den[:, c], rsum[:, c], esink[:, c], ALU.add))
                    st(dve.reciprocal(rden[:, c], (den if m == "swa" else rsum)[:, c]))
                    bank, out_sem = g.bank(JR[m][0] + h)
                    dve.tensor_tensor(yt[:, :, h * HD:(h + 1) * HD],
                                      bank[:, 0:TT * HD].rearrange("p (t d) -> p t d", t=TT),
                                      rden[:, c].unsqueeze(2).broadcast_to([P, TT, HD]), ALU.mult).then_inc(out_sem, 1)

                for n in range(UNITS + 5):
                    if n < UNITS:
                        h, b = divmod(n, TT)
                        nk = keys(m, b)[1]
                        dve.wait_ge(s_done[m], i * UNITS + n + 1)
                        ins = dve.tensor_reduce(nmax[:, n:n + 1], banks[2 + n % 4][:, 0:nk], AX_X, ALU.max, negate=True)
                        if m == "fox":
                            ins.then_inc(max_ready[m], 1)
                        else:
                            st(ins)
                            dve.tensor_tensor(nmax2[:, n:n + 1], nmax[:, n:n + 1], nsk8[:, h:h + 1],
                                              ALU.min).then_inc(max_ready[m], 1)
                    if 2 <= n < UNITS + 2:
                        attn_turn_out(dve, i, m, tr, n - 2)
                    if n >= 8 and n % 4 == 0:
                        head_out(n // 4 - 2)
                for j in (GH - 2, GH - 1):
                    g.wait_taken(dve, JR[m][0] + j)
                dve.tensor_tensor(yt, yt, gate, ALU.mult).then_inc(y_ready[m], 1)
                y_out(dve, i, m, tr, dst)
            st.leave(GROUPS)
            g.close(GROUPS, *JR[m]), tr.close(TR[m], GROUPS)

        def attn_pool(pool, st, m):
            if m == "fox":
                st(pool.memset(ones3, 1.0))
                st(pool.memset(c3g, 0.0))
                with pool.Fori(0, GROUPS) as i:
                    pool.wait_ge(probs[m], 1 + i * UNITS)
                    pool.dma_start(c3g[0:3, :, :], a["c3"][:, bass.ds(i * (GH * SEQ), GH * SEQ)].rearrange(
                        "c (h s) -> c h s", h=GH)).then_inc(c3_in, 16)
            else:
                pool.dma_start(cos_, a["cos"]).then_inc(rope_in, 16)
                pool.dma_start(sin_, a["sin"]).then_inc(rope_in, 16)
                pool.dma_start(sinkb, a["sinks"].broadcast_to([P, FOX_HEADS])).then_inc(rope_in, 16)
                with pool.Fori(0, GROUPS) as i:
                    pool.wait_ge(probs[m], 1 + i * UNITS)
                    pool.dma_start(w_kv, a["w_kv"][bass.ds(i, 1)].rearrange("o p k n -> p (o k) n")
                                   ).then_inc(wkv_in, 16)

        CT = HALF // P
        NH = HALF // HD
        wa_ready, sh_ready = sem("wa_ready"), sem("shifted")
        rw_in, sq_ready, cc_ready = sem("rw_params_in"), sem("kk_squared"), sem("decay_sums_ready")
        ea_in_ready, exps_ready, ea_ready = sem("decay_before_ready"), sem("exps_ready"), sem("decay_before_exp")
        bk_ready, bz_ready, rkr_ready = sem("b_and_k_ready"), sem("bz_and_kz_ready"), sem("rkr_ready")
        zsig, prep_done, round_done = sem("z_sigmoid"), sem("prep_done"), sem("rwkv_round_done")
        ch_done, ch_act, ch_dve = sem("chunk_products"), sem("chunk_out_act"), sem("chunk_out_dve")
        o_sq, o_root, o_ready = sem("o_var_ready"), sem("o_root"), sem("o_ready")
        vsh_ready = sem("v_shifted")
        rc_ = Carve(ws)
        kz, vtm, btm, ktm = rc_(CT, 2, SEQ), rc_(TT, HALF), rc_(TT, HALF), rc_(TT, HALF)
        sz, zsh, o_tm = rc_(CT, SEQ), rc_(CT, SEQ), rc_(TT, HALF)
        raw = [rc_(SEQ + 1) for _ in range(2)]
        rsh, ksh, vsh = rc_(CT, SEQ), rc_(CT, SEQ), rc_(CT, SEQ)
        bt, kt2_ = rc_(SEQ), rc_(SEQ)
        rw_mu = rc_(RW // HALF * CT * 4)
        par, gnw, gnb = rc_(CT, 5), rc_(HALF), rc_(HALF)
        up = rc_(2, HALF)
        wa, bones, bones2, reset = rc_(SEQ), rc_(P), rc_(2), rc_(SEQ)
        omka, gexp, bonus = rc_(CT), rc_(CT, NCH), rc_(TT, NH)
        osum, ovar, oroot, orstd = rc_(TT * NH), rc_(TT * NH), rc_(TT * NH), rc_(TT * NH)
        wa_mu = rc_(1)
        shared_at = rc_.at
        lw, cs_, cc, ep, em, ea, asg, kk, sq = [rc_(SEQ) for _ in range(9)]
        rc_.at = shared_at
        m4, xx, xt, wsb = rc_(NH, 4 * P), rc_(NH, P), rc_(NH, P), rc_(NH, P)
        r0s, us, stbd, stmp = rc_(HALF), rc_(HALF), rc_(CT, P), rc_(CT, P)
        bmask = small[:, 16:16 + P]
        rc_.at = shared_at
        w_wa = rc_(KT, P)
        rc2 = Carve(r2, 8 * SEQ)
        ar, bz = rc2(CT, NCH, 2, P), rc2(CT, 2, SEQ)
        W0, A0, K_K, K_A, R_K = range(5)
        wwa_in, bones_in = sem("w_wa_in"), sem("bones_in")

        def wa_pool(pool):
            pool.dma_start(w_wa, a["w_wa"]).then_inc(wwa_in, 16)
            pool.dma_start(wa_mu, a["wa_mu"]).then_inc(wwa_in, 16)
            for to, frm in ((bones, "bones"), (bones2, "bones2"), (bmask, "bones"), (reset, "reset"),
                            (rw_mu, "rw_mu")):
                pool.dma_start(to, a[frm]).then_inc(bones_in, 16)

        def wa_pe(pe, ht):
            pe.wait_ge(wwa_in, 32)
            g = Gemm(PE_T)
            small_weights(pe, g, w_wa, chan(ht), P, by_channel=True)
            g.close(1, 1, 1)

        held = sem("held")

        def keep_where(dve, to, mask, frm):
            dve.sem_inc(held, 1)
            return dve.copy_predicated(to, mask, frm)

        def shift(dve, st, rw, mu, to, scratch):
            st(dve.tensor_tensor(scratch, rw[:, 0:SEQ], rw[:, 1:SEQ + 1], ALU.subtract))
            return dve.scalar_tensor_tensor(to, scratch, mu, rw[:, 1:SEQ + 1], ALU.mult, ALU.add)

        def wa_dve(dve, st):
            dve.wait_ge(wwa_in, 32)
            for r in raw:
                st(dve.memset(r[:, 0:1], 0.0))
            g = Gemm(DVE_T)
            bank, out_sem = g.product(dve, 0)
            dve.tensor_copy(raw[0][:, 1:SEQ + 1], bank[:]).then_inc(out_sem, 1)
            g.wait_taken(dve, 0)
            g.close(1, 1, 1)
            shift(dve, st, raw[0], wa_mu[:, 0:1], wa, bt).then_inc(wa_ready, 1)

        def wa_act(act):
            g = Gemm(ACT_T)
            g.close(1, 1, 1)
            act.wait_ge(wa_ready, 1)
            act.activation(wa[0:RANK, :], wa[0:RANK, :], ACT.Tanh).then_inc(wa_ready, 1)

        ROUNDS = RW // HALF
        RJ, RT_ = (16, 16), 8
        CHUNK = [(f"G{h}", 2 + h % 2, "dve") for h in range(NH)] + [("L", 4, "dve")]
        for lv in range(1, LEVELS):
            CHUNK += [(f"W{lv}", 5, "act")] + [(f"X{lv}", 2, "dve")] * (lv < LEVELS - 1) + [(f"T{lv}", 3, "dve")]
        CHUNK += [("R", 4, "act"), ("U", 5, "dve"), ("O", 2, "act"), ("S", 3, "dve")]
        CN = {"pe": len(CHUNK), "act": sum(e == "act" for *_, e in CHUNK), "dve": sum(e == "dve" for *_, e in CHUNK)}
        CBANK = {name: banks[b] for name, b, _ in CHUNK}

        def ch_count(who, name):
            upto = [x for x, *_ in CHUNK].index(name) + 1
            return sum(who in ("pe", e) for _, _, e in CHUNK[:upto])

        def ch_wait(eng, who, i, c, name):
            s = {"pe": ch_done, "act": ch_act, "dve": ch_dve}[who]
            eng.wait_ge(s, 1 + at(i, NCH * CN[who], c * CN[who] + (ch_count(who, name) if name else 0)))

        def rwkv_pe(pe, ht):
            pe.wait_ge(bones_in, 80)
            pe.wait_ge(wa_ready, 2)
            g, sl = Gemm(PE_T), Slots()
            for _ in range(4):
                weights(pe, g, sl, chan(ht), HALF, by_channel=True)

            def round_(i, last):
                g, tr, sl = Gemm(PE_T, i, *RJ), Turns(PE_T, i, RT_), Slots(i, 8)
                g.u, sl.n = 8, SLOTS
                ahead = iter(()) if last else (x for _ in range(4) for x in weights_steps(
                    pe, g, sl, chan(ht), HALF, by_channel=True))

                def fill():
                    for _ in range(2):
                        next(ahead, None)

                pe.wait_ge(rw_in, i * 64 + 64)
                pe.wait_ge(vsh_ready, 1 + i * 2 + 2)
                for ct in range(CT):
                    bank = tr.claim(pe)
                    for t in range(TT):
                        mm = pe.transpose(bank[:, t * P:(t + 1) * P], vsh[:, ct, t * P:(t + 1) * P], ident[:])
                    mm.then_inc(tr_done, 1)
                for ct in range(CT):
                    for w in range(2):
                        bank = g.claim(pe)
                        pe.matmul(bank[:], up[:, w, ct * P:(ct + 1) * P], wa, start=True, stop=True).then_inc(gemm_done, 1)
                    pe.wait_ge(sq_ready, i * 2 + ct + 1)
                    bank = g.claim(pe)
                    pe.matmul(bank[:], bones, sq, start=True, stop=True).then_inc(gemm_done, 1)
                    pe.wait_ge(bk_ready, i * 4 + 2 * ct + 2)
                    for x in (bt, kt2_):
                        bank = tr.claim(pe)
                        for t in range(TT):
                            mm = pe.transpose(bank[:, t * P:(t + 1) * P], x[:, t * P:(t + 1) * P], ident[:])
                        mm.then_inc(tr_done, 1)
                    pe.wait_ge(rkr_ready, i * 2 + ct + 1)
                    bank = g.claim(pe)
                    for t in range(TT):
                        mm = pe.matmul(bank[:, 2 * t:2 * t + 2], sq[:, t * P:(t + 1) * P], bones2, start=True, stop=True)
                    mm.then_inc(gemm_done, 1)
                for n in (4, 5):
                    tr.wait_out(pe, n)
                pe.wait_ge(prep_done, 1 + i * 3 + 3)
                pe.wait_ge(bz_ready, i * 8 + 8)

                def four(name, lhs, rhs):
                    for h in range(NH):
                        mm = pe.matmul(CBANK[name][:, h * P:(h + 1) * P], lhs[:, h, 0:P], rhs[:, h, :], start=True, stop=True)
                    mm.then_inc(ch_done, 1)

                for c in range(NCH):
                    tk = slice(c * P, (c + 1) * P)
                    fill()
                    ch_wait(pe, "act", i, c, None)
                    ch_wait(pe, "dve", i, c, None)
                    for h in range(NH):
                        if h == 2:
                            fill()
                        if h >= 2:
                            ch_wait(pe, "dve", i, c, f"G{h - 2}")
                        bank = CBANK[f"G{h}"]
                        both_ = ar[:, h // 2, c, :, :].rearrange("p x t -> p (x t)")
                        pe.matmul(bank[:, 0:2 * P], bz[:, h // 2, h % 2, tk], both_, start=True, stop=True)
                        pe.matmul(bank[:, 2 * P:4 * P], kz[:, h // 2, h % 2, tk], both_, start=True,
                                  stop=True).then_inc(ch_done, 1)
                    for h in range(NH):
                        mm = pe.matmul(CBANK["L"][:, h * P:(h + 1) * P], ar[:, h // 2, c, 0, :], bz[:, h // 2, h % 2, tk],
                                       start=True, stop=True)
                    mm.then_inc(ch_done, 1)
                    for lv in range(1, LEVELS):
                        fill()
                        ch_wait(pe, "dve", i, c, f"T{lv - 1}" if lv > 1 else "L")
                        four(f"W{lv}", m4, xx)
                        fill()
                        ch_wait(pe, "act", i, c, f"W{lv}")
                        if lv < LEVELS - 1:
                            four(f"X{lv}", xt, wsb)
                        four(f"T{lv}", wsb, xt)
                    for ct in range(CT):
                        pe.matmul(CBANK["R"][:, ct * P:(ct + 1) * P], ar[:, ct, c, 0, :], stbd[:, ct, :], start=True, stop=False)
                        for h in (2 * ct, 2 * ct + 1):
                            mm = pe.matmul(CBANK["R"][:, h * HD:(h + 1) * HD], m4[:, h, 2 * P:3 * P],
                                           vtm[:, c, h * HD:(h + 1) * HD], start=False, stop=(h % 2 == 1))
                    mm.then_inc(ch_done, 1)
                    fill()
                    ch_wait(pe, "dve", i, c, f"T{LEVELS - 1}")
                    ch_wait(pe, "act", i, c, "R")
                    for h in range(NH):
                        mm = pe.matmul(CBANK["U"][:, h * HD:(h + 1) * HD], xt[:, h, :], r0s[:, h * HD:(h + 1) * HD],
                                       start=True, stop=True)
                    mm.then_inc(ch_done, 1)
                    fill()
                    ch_wait(pe, "dve", i, c, "U")
                    for ct in range(CT):
                        pe.matmul(CBANK["O"][:, ct * P:(ct + 1) * P], ar[:, ct, c, 1, :], stbd[:, ct, :], start=True, stop=False)
                        for h in (2 * ct, 2 * ct + 1):
                            hs = slice(h * HD, (h + 1) * HD)
                            pe.matmul(CBANK["O"][:, hs], m4[:, h, P:2 * P], us[:, hs], start=False, stop=False)
                            mm = pe.matmul(CBANK["O"][:, hs], m4[:, h, 3 * P:4 * P], vtm[:, c, hs],
                                           start=False, stop=(h % 2 == 1))
                    mm.then_inc(ch_done, 1)
                    for ct in range(CT):
                        cs = slice(ct * P, (ct + 1) * P)
                        pe.matmul(CBANK["S"][:, cs], btm[:, c, cs], us[:, cs], start=True, stop=False)
                        mm = pe.matmul(CBANK["S"][:, cs], ktm[:, c, cs], vtm[:, c, cs], start=False, stop=True)
                    mm.then_inc(ch_done, 1)
                assert next(ahead, None) is None
                pe.wait_ge(o_ready, i + 1)
                for ct in range(CT):
                    bank = tr.claim(pe)
                    for t in range(TT):
                        mm = pe.transpose(bank[:, t * P:(t + 1) * P], o_tm[:, t, ct * P:(ct + 1) * P], ident[:])
                    mm.then_inc(tr_done, 1)
                assert (g.u, tr.n) == (8 + (8 if last else 16), RT_), (g.u, tr.n)

            with pe.Fori(0, ROUNDS - 1) as i:
                round_(i, last=False)
            round_(ROUNDS - 1, last=True)
            g.close(ROUNDS, *RJ), sl.close(ROUNDS), Turns(PE_T).close(RT_, ROUNDS)

        def tok_out(eng, tr, n, to):
            bank, out_sem = tr.wait(eng, n)
            frm = bank[:].rearrange("p (t c) -> p t c", t=TT)
            (eng.tensor_copy(to, frm) if eng is nc.vector else eng.activation(to, frm, ACT.Copy)).then_inc(out_sem, 1)

        def raw_out(act, g, i, j, ahead=0):
            bank, out_sem = g.product(act, j + ahead)
            act.wait_ge(sh_ready, 1 + i * 6 + (0 if j < 2 else j - 1 if j < 5 else 4 if j == 5 else j - 3))
            act.wait_ge(vsh_ready, 1 + i * 2 + (0 if j < 6 else j - 5))
            act.activation(raw[j % 2][:, 1:SEQ + 1], bank[:], ACT.Copy).then_inc(out_sem, 1)

        AHEAD = {(c, lv): 2 * c + k for c in range(NCH) for k, lv in ((-1, 2), (0, 5)) if 2 * c + k >= 0}

        def rwkv_act(act, st, dst):
            g = Gemm(ACT_T)
            for j in range(8):
                raw_out(act, g, 0, j)

            def round_(i, last):
                g, tr = Gemm(ACT_T, i, *RJ), Turns(ACT_T, i, RT_)
                act.wait_ge(round_done, 1 + i)
                act.wait_ge(sh_ready, 1 + i * 6 + 6)
                act.activation(o_tm.rearrange("p t n -> p (t n)"), zsh.rearrange("p c s -> p (c s)"),
                               ACT.Sigmoid).then_inc(zsig, 1)
                act.wait_ge(rw_in, i * 64 + 64)
                tok_out(act, tr, 0, vtm[:, :, 0:P])
                for ct in range(CT):
                    act.wait_ge(prep_done, 1 + i * 3 + ct)
                    bank, out_sem = g.product(act, 8 + 4 * ct)
                    act.activation(cs_, bank[:], ACT.Sigmoid, bias=par[:, ct, W0:W0 + 1]).then_inc(out_sem, 1)
                    bank, out_sem = g.product(act, 9 + 4 * ct)
                    act.activation(asg, bank[:], ACT.Sigmoid, bias=par[:, ct, A0:A0 + 1]).then_inc(out_sem, 1)
                    bank, out_sem = g.product(act, 10 + 4 * ct)
                    act.activation(ep, bank[:], ACT.Sqrt).then_inc(out_sem, 1)
                    act.wait_ge(cc_ready, i * 4 + 2 * ct + 2)
                    act.activation(em, cc, ACT.Exp, scale=-1.0).then_inc(exps_ready, 1)
                    act.activation(gexp[:, ct, :], gexp[:, ct, :], ACT.Exp).then_inc(exps_ready, 1)
                    act.wait_ge(ea_in_ready, i * 2 + ct + 1)
                    act.activation(ea, ea, ACT.Exp).then_inc(exps_ready, 1)
                    act.wait_ge(rkr_ready, i * 2 + ct + 1)
                    act.activation(ep, cc, ACT.Exp).then_inc(exps_ready, 1)
                    act.wait_ge(bk_ready, i * 4 + 2 * ct + 2)
                    for to, frm in ((bz, bt), (kz, kt2_)):
                        for half in range(2):
                            hp = slice(half * HD, (half + 1) * HD)
                            act.activation(to[hp, ct, half, :], frm[hp, :], ACT.Copy).then_inc(bz_ready, 1)
                    cs = slice(ct * P, (ct + 1) * P)
                    tok_out(act, tr, 2 + 2 * ct, btm[:, :, cs])
                for c in range(NCH):
                    for lv in range(1, LEVELS):
                        ch_wait(act, "pe", i, c, f"W{lv}")
                        act.activation(wsb.rearrange("p h n -> p (h n)"), CBANK[f"W{lv}"][:], ACT.Copy).then_inc(ch_act, 1)
                        if not last and (c, lv) in AHEAD:
                            raw_out(act, g, i + 1, AHEAD[c, lv], 16)
                    ch_wait(act, "pe", i, c, "R")
                    act.activation(r0s, CBANK["R"][:, 0:HALF], ACT.Copy).then_inc(ch_act, 1)
                    ch_wait(act, "pe", i, c, "O")
                    act.activation(o_tm[:, c, :], CBANK["O"][:, 0:HALF], ACT.Copy).then_inc(ch_act, 1)
                if not last:
                    raw_out(act, g, i + 1, 7, 16)
                act.wait_ge(o_sq, i + 1)
                act.activation(oroot, ovar, ACT.Sqrt, bias=eps[GN_EPS], scale=1.0 / HD).then_inc(o_root, 1)
                bank, out_sem = tr.wait(act, 6)
                act.activation(chan(dst)[:, bass.ds(i * CT, 1), :].rearrange("p o s -> p (o s)"), bank[:],
                               ACT.Copy).then_inc(out_sem, 1)

            with act.Fori(0, ROUNDS - 1) as i:
                round_(i, last=False)
            round_(ROUNDS - 1, last=True)
            g.close(ROUNDS, *RJ), Turns(ACT_T).close(RT_, ROUNDS)

        def rwkv_dve(dve, st, dst):
            dve.wait_ge(bones_in, 80)
            for z in (bz, kz):
                st(dve.memset(z[0:HD, :, 1, :], 0.0))
                st(dve.memset(z[HD:P, :, 0, :], 0.0))
            to = [rsh, rsh, ksh, ksh, vsh, vsh, zsh, zsh]

            def shift_in(g, i, j, ahead=0):
                g.wait_taken(dve, j + ahead)
                if j:
                    dve.wait_ge(vsh_ready if 5 <= j <= 6 else sh_ready,
                                1 + (i * 2 + (j - 4) if 5 <= j <= 6 else i * 6 + (j if j < 5 else j - 2)))
                shift(dve, st, raw[j % 2], rw_mu[:, bass.ds(i * (4 * CT) + ((j % 2) * 4 + j // 2), 1)],
                      to[j][:, j % 2, :], bt).then_inc(vsh_ready if j // 2 == 2 else sh_ready, 1)

            g = Gemm(DVE_T)
            for j in range(8):
                shift_in(g, 0, j)

            def round_(i, last):
                g, tr = Gemm(DVE_T, i, *RJ), Turns(DVE_T, i, RT_)
                dve.wait_ge(rw_in, i * 64 + 64)
                dve.wait_ge(sh_ready, 1 + i * 6 + 6)
                dve.wait_ge(zsig, i + 1)
                st(dve.tensor_tensor(sz.rearrange("p c s -> p (c s)"), zsh.rearrange("p c s -> p (c s)"),
                                     o_tm.rearrange("p t n -> p (t n)"), ALU.mult))
                tok_out(dve, tr, 1, vtm[:, :, P:2 * P])
                st(dve.tensor_scalar(omka, par[:, :, K_A], -1.0, 1.0, ALU.mult, ALU.add))
                for ct in range(CT):
                    pc = [par[:, ct, x:x + 1] for x in range(5)]
                    g.wait_taken(dve, 8 + 4 * ct)
                    st(dve.tensor_scalar(lw, cs_, -EXP_HALF, None, ALU.mult))
                    st(dve.tensor_tensor_scan(cs_, reset, lw, 0.0, ALU.mult, ALU.add))
                    c3v = cs_.rearrange("p (c t) -> p c t", c=NCH)
                    ccv = cc.rearrange("p (c t) -> p c t", c=NCH)
                    mid = CH // 2 - 1
                    dve.tensor_tensor(ccv, c3v, c3v[:, :, mid:mid + 1].broadcast_to([P, NCH, CH]),
                                      ALU.subtract).then_inc(cc_ready, 1)
                    dve.wait_ge(cc_ready, i * 4 + 2 * ct + 1)
                    st(dve.tensor_copy(gexp[:, ct, NCH - 1:NCH], cc[:, SEQ - 1:SEQ]))
                    dve.tensor_tensor(gexp[:, ct, 0:NCH - 1], ccv[:, 0:NCH - 1, CH - 1], c3v[:, 1:NCH, mid],
                                      ALU.add).then_inc(cc_ready, 1)
                    dve.tensor_tensor(ea, cc, lw, ALU.subtract).then_inc(ea_in_ready, 1)
                    st(dve.tensor_scalar(kk, ksh[:, ct, :], pc[K_K], None, ALU.mult))
                    if ct:
                        dve.wait_ge(gemm_done, at(i, RJ[0], DVE_T.jobs + 12))
                    dve.tensor_tensor(sq, kk, kk, ALU.mult).then_inc(sq_ready, 1)
                    g.wait_taken(dve, 10 + 4 * ct)
                    st(dve.tensor_scalar(sq, ep, 1e-12, None, ALU.max))
                    st(dve.reciprocal(sq, sq))
                    st(dve.tensor_tensor(kk, kk, sq, ALU.mult))
                    g.wait_taken(dve, 9 + 4 * ct)
                    st(dve.tensor_scalar(sq, asg, pc[K_A], omka[:, ct:ct + 1], ALU.mult, ALU.add))
                    st(dve.tensor_tensor(ksh[:, ct, :], ksh[:, ct, :], sq, ALU.mult))
                    st(dve.scalar_tensor_tensor(sq, rsh[:, ct, :], pc[R_K], ksh[:, ct, :], ALU.mult, ALU.mult))
                    dve.sem_inc(rkr_ready, 1)
                    dve.wait_ge(exps_ready, i * 8 + 4 * ct + 4)
                    kkv, eav = kk.rearrange("p (c t) -> p c t", c=NCH), ea.rearrange("p (c t) -> p c t", c=NCH)
                    st(dve.scalar_tensor_tensor(ar[:, ct, :, 0, :], kkv, -1.0, eav, ALU.mult, ALU.mult))
                    st(dve.tensor_tensor(ar[:, ct, :, 1, :], rsh[:, ct, :].rearrange("p (c t) -> p c t", c=NCH),
                                         ep.rearrange("p (c t) -> p c t", c=NCH), ALU.mult))
                    st(dve.tensor_tensor(kk, kk, asg, ALU.mult))
                    if ct:
                        dve.wait_ge(bz_ready, i * 8 + 4)
                        dve.wait_ge(tr_done, at(i, RT_, DVE_T.turns + 4))
                    dve.tensor_tensor(bt, kk, em, ALU.mult).then_inc(bk_ready, 1)
                    dve.tensor_tensor(kt2_, ksh[:, ct, :], em, ALU.mult).then_inc(bk_ready, 1)
                    bank, out_sem = g.product(dve, 11 + 4 * ct)
                    dve.tensor_copy(bonus[:, :, 2 * ct:2 * ct + 2], bank[:, 0:2 * TT].rearrange("p (t h) -> p t h", t=TT)
                                    ).then_inc(out_sem, 1)
                    tok_out(dve, tr, 3 + 2 * ct, ktm[:, :, ct * P:(ct + 1) * P])
                    dve.wait_ge(bk_ready, i * 4 + 2 * ct + 2)
                    dve.sem_inc(prep_done, 1)
                dve.wait_ge(bz_ready, i * 8 + 8)
                st(dve.memset(m4, 0.0))
                st(dve.memset(stbd, 0.0))
                dve.sem_inc(prep_done, 1)
                idb = ident[:].unsqueeze(1).broadcast_to([P, NH, P])
                for c in range(NCH):
                    ch_wait(dve, "pe", i, c, None)
                    st(dve.tensor_copy(xx, idb))
                    st(dve.tensor_copy(xt, idb))

                    def merge(to, mask, name):
                        return keep_where(dve, to, mask.unsqueeze(1).broadcast_to([P, NH, P]),
                                                   CBANK[name][:].rearrange("p (h n) -> p h n", h=NH))

                    for h in range(NH):
                        ch_wait(dve, "pe", i, c, f"G{h}")
                        keep_where(dve, m4[:, h, :], tril4[:], CBANK[f"G{h}"][:]).then_inc(ch_dve, 1)
                    ch_wait(dve, "dve", i, c, f"G{NH - 1}")
                    st(keep_where(dve, xt, lmaskt[:, 0, :].unsqueeze(1).broadcast_to([P, NH, P]), m4[:, :, 0:P]))
                    ch_wait(dve, "pe", i, c, "L")
                    merge(xx, lmask[:, 0, :], "L").then_inc(ch_dve, 1)
                    for lv in range(1, LEVELS):
                        if lv < LEVELS - 1:
                            ch_wait(dve, "pe", i, c, f"X{lv}")
                            merge(xx, lmask[:, lv, :], f"X{lv}").then_inc(ch_dve, 1)
                        ch_wait(dve, "pe", i, c, f"T{lv}")
                        merge(xt, lmaskt[:, lv, :], f"T{lv}").then_inc(ch_dve, 1)
                        if not last and (c, lv) in AHEAD:
                            shift_in(g, i + 1, AHEAD[c, lv], 16)
                    ch_wait(dve, "pe", i, c, "U")
                    dve.tensor_copy(us, CBANK["U"][:, 0:HALF]).then_inc(ch_dve, 1)
                    ch_wait(dve, "pe", i, c, "S")
                    st(dve.tensor_tensor(stmp, stbd, CBANK["S"][:, 0:HALF].rearrange("p (c n) -> p c n", c=CT), ALU.add))
                    st(dve.scalar_tensor_tensor(stbd[:, 0, :], stmp[:, 0, :], gexp[:, 0, c:c + 1], bmask, ALU.mult, ALU.mult))
                    dve.scalar_tensor_tensor(stbd[:, 1, :], stmp[:, 1, :], gexp[:, 1, c:c + 1], bmask,
                                             ALU.mult, ALU.mult).then_inc(ch_dve, 1)
                if not last:
                    shift_in(g, i + 1, 7, 16)
                ch_wait(dve, "act", i, NCH - 1, "S")
                o3 = o_tm.rearrange("p t (h d) -> p (t h) d", h=NH)
                sh = [P, TT * NH, HD]
                tmp = m4.rearrange("p h n -> p (h n)")[:, 0:TT * HALF].rearrange("p (x d) -> p x d", d=HD)
                st(dve.tensor_reduce(osum, o3, AX_X, ALU.add))
                st(dve.tensor_scalar(osum, osum, 1.0 / HD, None, ALU.mult))
                st(dve.tensor_tensor(o3, o3, osum.unsqueeze(2).broadcast_to(sh), ALU.subtract))
                ch_wait(dve, "pe", i, NCH - 1, "S")
                st(dve.tensor_tensor(tmp, o3, o3, ALU.mult))
                dve.tensor_reduce(ovar, tmp, AX_X, ALU.add).then_inc(o_sq, 1)
                dve.wait_ge(o_root, i + 1)
                st(dve.reciprocal(orstd, oroot))
                st(dve.tensor_tensor(o3, o3, orstd.unsqueeze(2).broadcast_to(sh), ALU.mult))
                st(dve.tensor_tensor(o_tm, o_tm, gnw.unsqueeze(1).broadcast_to([P, TT, HALF]), ALU.mult))
                st(dve.tensor_tensor(o_tm, o_tm, gnb.unsqueeze(1).broadcast_to([P, TT, HALF]), ALU.add))
                st(dve.tensor_tensor(tmp, vtm.rearrange("p t (h d) -> p (t h) d", h=NH),
                                     bonus.rearrange("p t h -> p (t h)").unsqueeze(2).broadcast_to(sh), ALU.mult))
                dve.tensor_tensor(o3, o3, tmp, ALU.add).then_inc(o_ready, 1)
                bank, out_sem = tr.wait(dve, 7)
                o_t = chan(dst)[:, bass.ds(i * CT, CT), :]
                dve.tensor_copy(chan(dst)[:, bass.ds(i * CT + 1, 1), :].rearrange("p o s -> p (o s)"), bank[:]).then_inc(out_sem, 1)
                tr.wait_out(dve, 6)
                tr.wait_out(dve, 7)
                dve.tensor_tensor(o_t, o_t, sz, ALU.mult).then_inc(round_done, 1)

            with dve.Fori(0, ROUNDS - 1) as i:
                st.enter(i, 67)
                round_(i, last=False)
            st.leave(ROUNDS - 1)
            round_(ROUNDS - 1, last=True)
            g.close(ROUNDS, *RJ), Turns(DVE_T).close(RT_, ROUNDS)

        def rwkv_pool(pool):
            with pool.Fori(0, ROUNDS) as i:
                pool.wait_ge(round_done, 1 + i)
                def row(name):
                    return a[name][bass.ds(i, 1)]
                pool.dma_start(par, row("rw_par").rearrange("o p c n -> p (o c) n")).then_inc(rw_in, 16)
                pool.dma_start(up, row("rw_up").rearrange("o p c n -> p (o c) n")).then_inc(rw_in, 16)
                pool.dma_start(gnw, row("gn_w").broadcast_to([P, HALF])).then_inc(rw_in, 16)
                pool.dma_start(gnb, row("gn_b").broadcast_to([P, HALF])).then_inc(rw_in, 16)

        HJ, HT = (10, 10), 4
        hp_in, h_sig, h_qs = sem("hgrn_params_in"), sem("h_sigmoid"), sem("h_q_ready")
        h_lf, h_ln, h_b, h_exp, h_dif = sem("h_log_in"), sem("h_log_out"), sem("h_sums"), sem("h_exps"), sem("h_level_in")
        h_lexp, h_mix, h_att, h_att_out = sem("h_level_exp"), sem("h_mix_ready"), sem("h_att_done"), sem("h_att_out")
        h_kd, h_prod, h_o, h_s = sem("h_kd_ready"), sem("h_products"), sem("h_o_out"), sem("h_state_out")
        h_sq, h_root, h_ready, h_done, h_begin = (sem("h_sq_ready"), sem("h_root"), sem("h_ready"), sem("hgrn_round_done"),
                                                  sem("h_zeroed"))
        hc = Carve(ws)
        qs, hk, hz, hb, hf, hl, he = [hc(CT, SEQ) for _ in range(7)]
        qe, kd, kdtm, itm, ho = hc(CT, SEQ), hc(CT, SEQ), hc(TT, HALF), hc(TT, HALF), hc(TT, HALF)
        mix = [hc(CT, SEQ) for _ in range(2)]
        att = hc(CT, NCH, CH)
        hs_ = hc(CT, P)
        hgl = hc(CT, NCH)
        hpar, lbc = hc(CT, 2), hc(CT, 8)
        hss, hroot, hrstd = hc(TT * CT), hc(TT * CT), hc(TT * CT)
        hreset = hc(SEQ)
        LB, OML, LLB, L1M = 4, 5, 6, 7

        def flat(x):
            return x.rearrange("p c s -> p (c s)")

        def hgrn_pool(pool):
            pool.dma_start(hreset, a["reset"]).then_inc(hp_in, 16)
            with pool.Fori(0, ROUNDS) as i:
                pool.wait_ge(h_done, 1 + i)
                pool.dma_start(hpar, a["hg_par"][bass.ds(i, 1)].rearrange("o p c n -> p (o c) n")).then_inc(hp_in, 16)

        def hgrn_pe(pe, ht):
            with pe.Fori(0, ROUNDS) as i:
                g, tr, sl = Gemm(PE_T, i, *HJ), Turns(PE_T, i, HT), Slots(i, 8)
                weights(pe, g, sl, chan(ht), HALF, by_channel=True)
                weights(pe, g, sl, chan(ht), HALF, by_channel=True)
                weights(pe, g, sl, chan(ht), HALF, by_channel=False)
                weights(pe, g, sl, chan(ht), HALF, by_channel=True)
                pe.wait_ge(h_begin, i + 1)
                for lv in range(LEVELS + 1):
                    for ct in range(CT):
                        n = CT * lv + ct
                        pe.wait_ge(h_att_out, 1 + i * 16 + max(0, n - 1))
                        if lv < LEVELS:
                            pe.wait_ge(h_mix, i * 14 + 2 * lv + 2)
                        else:
                            pe.wait_ge(h_qs, i * 2 + 2)
                        for c in range(NCH):
                            tk = slice(c * P, (c + 1) * P)
                            lhs, rhs = (mix[lv % 2], mix[lv % 2]) if lv < LEVELS else (hk, qs)
                            mm = pe.matmul(banks[2 + n % 2][:, tk], lhs[:, ct, tk], rhs[:, ct, tk], start=True, stop=True)
                        mm.then_inc(h_att, 1)
                pe.wait_ge(h_kd, i * 2 + 2)
                for ct in range(CT):
                    bank = tr.claim(pe)
                    for t in range(TT):
                        mm = pe.transpose(bank[:, t * P:(t + 1) * P], kd[:, ct, t * P:(t + 1) * P], ident[:])
                    mm.then_inc(tr_done, 1)
                pe.wait_ge(h_att_out, 1 + i * 16 + 16)
                for j in (6, 7):
                    g.wait_taken(pe, j)
                for n in range(2):
                    tr.wait_out(pe, n)
                for c in range(NCH):
                    pe.wait_ge(h_s, 1 + i * NCH + c)
                    pe.wait_ge(h_o, 1 + i * NCH + c)
                    for ct in range(CT):
                        cs = slice(ct * P, (ct + 1) * P)
                        pe.matmul(banks[4][:, cs], qe[:, ct, c * P:(c + 1) * P], hs_[:, ct, :], start=True, stop=False)
                        mm = pe.matmul(banks[4][:, cs], att[:, ct, c, :], itm[:, c, cs], start=False, stop=True)
                    mm.then_inc(h_prod, 1)
                    for ct in range(CT):
                        cs = slice(ct * P, (ct + 1) * P)
                        mm = pe.matmul(banks[5][:, cs], kdtm[:, c, cs], itm[:, c, cs], start=True, stop=True)
                    mm.then_inc(h_prod, 1)
                pe.wait_ge(h_ready, i + 1)
                for ct in range(CT):
                    bank = tr.claim(pe)
                    for t in range(TT):
                        mm = pe.transpose(bank[:, t * P:(t + 1) * P], ho[:, t, ct * P:(ct + 1) * P], ident[:])
                    mm.then_inc(tr_done, 1)
                assert (g.u, tr.n) == (HJ[1], HT)
            g.close(ROUNDS, *HJ), sl.close(ROUNDS), tr.close(HT, ROUNDS)

        def hgrn_act(act, st, dst):
            with act.Fori(0, ROUNDS) as i:
                g, tr = Gemm(ACT_T, i, *HJ), Turns(ACT_T, i, HT)
                st.enter(i, 4)
                act.wait_ge(h_done, 1 + i)
                for ct in range(CT):
                    bank, _ = g.product(act, ct)
                    act.activation(qs[:, ct, :], bank[:], ACT.Sigmoid).then_inc(h_sig, 1)
                for ct in range(CT):
                    bank, out_sem = g.product(act, 2 + ct)
                    st(act.activation(hk[:, ct, :], bank[:], ACT.Sigmoid, scale=-1.0))
                    act.activation(hf[:, ct, :], bank[:], ACT.Copy).then_inc(out_sem, 1)
                for t in range(TT):
                    bank, out_sem = g.product(act, 4 + t)
                    act.activation(itm[:, t, :], bank[:, 0:HALF], ACT.Copy).then_inc(out_sem, 1)
                act.wait_ge(h_lf, i * 6 + 1)
                act.activation(lbc[:, :, 1], lbc[:, :, 0], ACT.Exp).then_inc(h_ln, 1)
                act.wait_ge(h_lf, i * 6 + 3)
                act.activation(lbc[:, :, LLB], lbc[:, :, LLB], ACT.Ln).then_inc(h_ln, 1)
                act.activation(lbc[:, :, L1M], lbc[:, :, OML], ACT.Ln).then_inc(h_ln, 1)
                act.wait_ge(h_lf, i * 6 + 4)
                st(act.activation(flat(hl), flat(hl), ACT.Exp, scale=-1.0))
                act.activation(flat(hl), flat(hl), ACT.Ln, bias=1.0).then_inc(h_ln, 1)
                act.wait_ge(h_lf, i * 6 + 6)
                st(act.activation(flat(hl), flat(hl), ACT.Exp, scale=-1.0))
                act.activation(flat(hl), flat(hl), ACT.Ln, bias=1.0).then_inc(h_ln, 1)
                act.wait_ge(h_b, i * 3 + 3)
                act.activation(flat(qe), flat(hb), ACT.Exp).then_inc(h_exp, 1)
                act.activation(flat(kd), flat(kd), ACT.Exp).then_inc(h_exp, 1)
                act.activation(flat(hgl), flat(hgl), ACT.Exp).then_inc(h_exp, 1)
                for lv in range(LEVELS):
                    act.wait_ge(h_dif, i * 14 + 2 * lv + 2)
                    act.activation(flat((he, hl)[lv % 2]), flat((he, hl)[lv % 2]), ACT.Exp).then_inc(h_lexp, 1)
                for ct in range(CT):
                    bank, _ = g.product(act, 8 + ct)
                    act.activation(hf[:, ct, :], bank[:], ACT.Sigmoid).then_inc(h_sig, 1)
                tok_out(act, tr, 0, kdtm[:, :, 0:P])
                for c in range(NCH):
                    act.wait_ge(h_prod, i * 8 + 2 * c + 1)
                    act.activation(ho[:, c, :], banks[4][:, 0:HALF], ACT.Copy).then_inc(h_o, 1)
                act.wait_ge(h_sq, i + 1)
                act.activation(hroot, hss, ACT.Sqrt, bias=eps[HGRN_EPS], scale=1.0 / P).then_inc(h_root, 1)
                bank, out_sem = tr.wait(act, 2)
                act.activation(chan(dst)[:, bass.ds(i * CT + 8, 1), :].rearrange("p o s -> p (o s)"), bank[:],
                               ACT.Copy).then_inc(out_sem, 1)
            st.leave(ROUNDS)
            g.close(ROUNDS, *HJ), tr.close(HT, ROUNDS)

        def hgrn_dve(dve, st, dst):
            st(dve.memset(flat(att.rearrange("p c n t -> p c (n t)")), 0.0))
            with dve.Fori(0, ROUNDS) as i:
                g, tr = Gemm(DVE_T, i, *HJ), Turns(DVE_T, i, HT)
                st.enter(i, 23)
                dve.wait_ge(hp_in, i * 16 + 32)
                dve.memset(flat(hs_), 0.0).then_inc(h_begin, 1)
                for ct in range(CT):
                    bank, out_sem = g.bank(ct)
                    dve.wait_ge(h_sig, i * 4 + ct + 1)
                    dve.tensor_tensor(qs[:, ct, :], qs[:, ct, :], bank[:], ALU.mult).then_inc(out_sem, 1)
                dve.tensor_tensor(lbc[:, :, 0], hpar[:, :, 0], hpar[:, :, 0], ALU.subtract).then_inc(h_lf, 1)
                dve.wait_ge(h_ln, i * 5 + 1)
                st(dve.reciprocal(lbc[:, :, 2], lbc[:, :, 1]))
                st(dve.tensor_tensor(lbc[:, :, 3], lbc[:, :, 1], lbc[:, :, 2], ALU.mult))
                st(dve.tensor_tensor(lbc[:, :, LB], lbc[:, :, 3], lbc[:, :, 3], ALU.subtract))
                dve.tensor_scalar(lbc[:, :, OML], lbc[:, :, LB], -1.0, 1.0, ALU.mult, ALU.add).then_inc(h_lf, 1)
                dve.tensor_scalar(lbc[:, :, LLB], lbc[:, :, LB], LB_FLOOR, LB_SCALE, ALU.max, ALU.mult).then_inc(h_lf, 1)
                dve.wait_ge(h_ln, i * 5 + 3)
                st(dve.tensor_scalar(lbc[:, :, LLB], lbc[:, :, LLB], -float(np.log(LB_SCALE)), None, ALU.add))
                for j in (2, 3):
                    g.wait_taken(dve, j)
                st(dve.tensor_scalar(flat(hl), flat(hf), -1.0, None, ALU.mult))
                dve.tensor_tensor(flat(hl), flat(hl), flat(hf), ALU.max).then_inc(h_lf, 1)
                for ct in range(CT):
                    dve.tensor_scalar(hk[:, ct, :], hk[:, ct, :], lbc[:, ct, OML:OML + 1], None, ALU.mult).then_inc(h_qs, 1)
                st(dve.tensor_scalar(flat(hf), flat(hf), 0.0, None, ALU.min))
                dve.wait_ge(h_ln, i * 5 + 4)
                st(dve.tensor_tensor(flat(hf), flat(hf), flat(hl), ALU.subtract))
                for ct in range(CT):
                    st(dve.tensor_scalar(hf[:, ct, :], hf[:, ct, :], lbc[:, ct, L1M:L1M + 1], None, ALU.add))
                for ct in range(CT):
                    st(dve.tensor_scalar(hl[:, ct, :], hf[:, ct, :], lbc[:, ct, LLB:LLB + 1], None, ALU.subtract))
                    st(dve.tensor_scalar(hf[:, ct, :], hf[:, ct, :], lbc[:, ct, LLB:LLB + 1], None, ALU.max))
                st(dve.tensor_scalar(flat(he), flat(hl), -1.0, None, ALU.mult))
                dve.tensor_tensor(flat(hl), flat(hl), flat(he), ALU.max).then_inc(h_lf, 1)
                dve.sem_inc(h_lf, 1)
                dve.wait_ge(h_ln, i * 5 + 5)
                st(dve.tensor_tensor(flat(hf), flat(hf), flat(hl), ALU.add))
                for ct in range(CT):
                    dve.tensor_tensor_scan(hb[:, ct, :], hreset, hf[:, ct, :], 0.0, ALU.mult, ALU.add).then_inc(h_b, 1)
                dve.wait_ge(h_b, i * 3 + 2)
                b8 = flat(hb).rearrange("p (n t) -> p n t", t=CH)
                st(dve.tensor_copy(hgl.rearrange("p c n -> p (c n)"), b8[:, :, CH - 1]))
                dve.tensor_tensor(flat(kd).rearrange("p (n t) -> p n t", t=CH), b8[:, :, CH - 1:CH].broadcast_to(
                    [P, CT * NCH, CH]), b8, ALU.subtract).then_inc(h_b, 1)

                def level_in(lv):
                    mlen = 1 << lv
                    n = CT * SEQ // (2 * mlen)
                    v = flat(hb).rearrange("p (n x t) -> p n x t", n=n, x=2)
                    e = flat((he, hl)[lv % 2]).rearrange("p (n x t) -> p n x t", n=n, x=2)
                    ref = v[:, :, 0, mlen - 1:mlen].broadcast_to([P, n, mlen])
                    dve.tensor_tensor(e[:, :, 1, :], v[:, :, 1, :], ref, ALU.subtract).then_inc(h_dif, 1)
                    dve.tensor_tensor(e[:, :, 0, :], ref, v[:, :, 0, :], ALU.subtract).then_inc(h_dif, 1)

                def level_mix(lv):
                    mlen = 1 << lv
                    n = CT * SEQ // (2 * mlen)
                    e, mx, q_, k_ = [flat(x).rearrange("p (n x t) -> p n x t", n=n, x=2)
                                     for x in ((he, hl)[lv % 2], mix[lv % 2], qs, hk)]
                    dve.wait_ge(h_lexp, i * 7 + lv + 1)
                    if lv >= 2:
                        dve.wait_ge(h_att, i * 16 + 2 * lv - 2)
                    dve.tensor_tensor(mx[:, :, 1, :], q_[:, :, 1, :], e[:, :, 1, :], ALU.mult).then_inc(h_mix, 1)
                    dve.tensor_tensor(mx[:, :, 0, :], k_[:, :, 0, :], e[:, :, 0, :], ALU.mult).then_inc(h_mix, 1)

                def level_out(lv):
                    for ct in range(CT):
                        n = CT * lv + ct
                        dve.wait_ge(h_att, i * 16 + n + 1)
                        keep_where(dve, att[:, ct, :, :], lmaskt[:, lv, :].unsqueeze(1).broadcast_to([P, NCH, CH]),
                                            banks[2 + n % 2][:].rearrange("p (n t) -> p n t", n=NCH)).then_inc(h_att_out, 1)

                dve.wait_ge(h_qs, i * 2 + 2)
                level_in(0)
                for lv in range(LEVELS):
                    if lv + 1 < LEVELS:
                        if lv >= 1:
                            dve.wait_ge(h_mix, i * 14 + 2 * lv)
                        level_in(lv + 1)
                    level_mix(lv)
                    if lv >= 1:
                        level_out(lv - 1)
                level_out(LEVELS - 1)
                level_out(LEVELS)
                dve.wait_ge(h_exp, i * 3 + 3)
                st(dve.tensor_tensor(flat(qe), flat(qe), flat(qs), ALU.mult))
                dve.tensor_tensor(flat(kd), flat(kd), flat(hk), ALU.mult).then_inc(h_kd, 1)
                dve.sem_inc(h_kd, 1)
                for ct in range(CT):
                    bank, out_sem = g.bank(8 + ct)
                    dve.wait_ge(h_sig, i * 4 + 2 + ct + 1)
                    dve.scalar_tensor_tensor(hz[:, ct, :], hf[:, ct, :], hpar[:, ct, 1:2], bank[:],
                                             ALU.mult, ALU.mult).then_inc(out_sem, 1)
                tok_out(dve, tr, 1, kdtm[:, :, P:2 * P])
                for c in range(NCH):
                    dve.wait_ge(h_prod, i * 8 + 2 * c + 2)
                    for ct in range(CT):
                        ins = dve.scalar_tensor_tensor(hs_[:, ct, :], hs_[:, ct, :], hgl[:, ct, c:c + 1],
                                                       banks[5][:, ct * P:(ct + 1) * P], ALU.mult, ALU.add)
                        ins.then_inc(h_s, 1) if ct else st(ins)
                dve.wait_ge(h_o, 1 + i * NCH + NCH)
                h3 = ho.rearrange("p t (h d) -> p (t h) d", h=CT)
                m3 = flat(mix[0]).rearrange("p (x d) -> p x d", d=P)
                st(dve.tensor_tensor(m3, h3, h3, ALU.mult))
                dve.tensor_reduce(hss, m3, AX_X, ALU.add).then_inc(h_sq, 1)
                dve.wait_ge(h_root, i + 1)
                st(dve.reciprocal(hrstd, hroot))
                dve.tensor_tensor(h3, h3, hrstd.unsqueeze(2).broadcast_to([P, TT * CT, P]), ALU.mult).then_inc(h_ready, 1)
                bank, out_sem = tr.wait(dve, 3)
                o_t = chan(dst)[:, bass.ds(i * CT + 8, CT), :]
                dve.tensor_copy(chan(dst)[:, bass.ds(i * CT + 9, 1), :].rearrange("p o s -> p (o s)"), bank[:]).then_inc(out_sem, 1)
                tr.wait_out(dve, 2)
                tr.wait_out(dve, 3)
                for j in (8, 9):
                    g.wait_taken(dve, j)
                dve.tensor_tensor(o_t, o_t, hz, ALU.mult).then_inc(h_done, 1)
            st.leave(ROUNDS)
            g.close(ROUNDS, *HJ), tr.close(HT, ROUNDS)

        ln_in, ln_var, ln_root, ln_ready, ln_out = (sem("ln_in"), sem("ln_var"), sem("ln_root"), sem("ln_ready"),
                                                    sem("out_stored"))
        lc = Carve(ws)
        ln_w, ln_b = lc(D), lc(D)
        stats, mv, lroot, lrstd = lc(TT, 4, 6), lc(TT, 2), lc(TT), lc(TT)

        def ln_pool(pool):
            pool.dma_start(ln_w, a["ln"][0:1, :].broadcast_to([P, D])).then_inc(ln_in, 16)
            pool.dma_start(ln_b, a["ln"][1:2, :].broadcast_to([P, D])).then_inc(ln_in, 16)

        def ln_dve(dve, st, src):
            s = tok(src)
            for t in range(TT):
                for k in range(4):
                    ins = dve.bn_stats(stats[:, t, k, :], s[:, t, k * N:(k + 1) * N])
                    st(ins)
                dve.bn_aggr(mv[:, t, :], stats[:, t, :, :]).then_inc(ln_var, 1)
            dve.wait_ge(ln_root, 1)
            st(dve.reciprocal(lrstd, lroot))
            dve.wait_ge(ln_in, 32)
            for t in range(TT):
                st(dve.tensor_scalar(s[:, t, :], s[:, t, :], mv[:, t, 0:1], lrstd[:, t:t + 1], ALU.subtract, ALU.mult))
                st(dve.tensor_tensor(s[:, t, :], s[:, t, :], ln_w, ALU.mult))
                dve.tensor_tensor(s[:, t, :], s[:, t, :], ln_b, ALU.add).then_inc(ln_ready, 1)

        def ln_act(act):
            act.wait_ge(ln_var, TT)
            act.activation(lroot, mv[:, :, 1], ACT.Sqrt, bias=eps[LN_EPS]).then_inc(ln_root, 1)

        block = ctx.enter_context(nc.Block())

        @block.sync
        def _(sp):
            for to, frm in ((ident[:], "ident"), (identb[:], "identb"), (maskb[:], "maskb"), (masks, "masks"),
                            (small[:, 12:16], "eps")):
                sp.dma_start(to, a[frm]).then_inc(consts_in, 16)
            for s in [*taken, *probs.values(), *y_ready.values(), *av_done.values(), sh_ready, vsh_ready, prep_done,
                      round_done, h_done, h_att_out, h_s, h_o, ch_done, ch_act, ch_dve]:
                sp.sem_inc(s, 1)
            sp.sem_inc(out_taken, 8)
            for s in range(SLOTS):
                sp.dma_start(wring[:, s, :], a["w"][s]).then_inc(w_full[s], 16)
            with sp.Fori(1, ALL_SLOTS // SLOTS) as i:
                for s in range(SLOTS):
                    sp.wait_ge(w_free, i * SLOTS + (s - 6))
                    sp.dma_start(wring[:, s, :], a["w"][bass.ds(i * SLOTS + s, 1)].rearrange("o p n -> p (o n)")
                                 ).then_inc(w_full[s], 16)
            for t in range(TT):
                sp.wait_ge(ln_ready, t + 1)
                sp.dma_start(out[t * P:(t + 1) * P, :], tok(r1)[:, t, :]).then_inc(ln_out, 16)
            sp.wait_ge(ln_out, 16 * TT)

        CONSTS = 5 * 16

        @block.tensor
        def _(pe):
            pe.wait_ge(consts_in, CONSTS)
            norm_pe(pe, 0), barrier("pe", pe)
            forget_pe(pe, r1), barrier("pe", pe)
            attn_pe(pe, "fox", r1), barrier("pe", pe)
            outp_pe(pe, 0, r2_split), barrier("pe", pe)
            norm_pe(pe, 1), barrier("pe", pe)
            attn_pe(pe, "swa", r2), barrier("pe", pe)
            outp_pe(pe, 1, r1_split), barrier("pe", pe)
            norm_pe(pe, 2), barrier("pe", pe)
            wa_pe(pe, r1)
            rwkv_pe(pe, r1), barrier("pe", pe)
            hgrn_pe(pe, r1), barrier("pe", pe)
            outp_pe(pe, 2, r2_split), barrier("pe", pe)

        @block.scalar
        def _(act):
            act.wait_ge(consts_in, CONSTS)
            st = Steps(act, act_step)
            norm_act(act, st, 0, r2, r1), barrier("act", act)
            forget_act(act), Gemm(ACT_T).close(1, 1, 1), barrier("act", act)
            attn_act(act, st, "fox", r2), barrier("act", act)
            outp_act(act, 0, r2), barrier("act", act)
            norm_act(act, st, 1, r1, r2), barrier("act", act)
            attn_act(act, st, "swa", r1), barrier("act", act)
            outp_act(act, 1, r1), barrier("act", act)
            norm_act(act, st, 2, r2, r1), barrier("act", act)
            wa_act(act)
            rwkv_act(act, st, r2), barrier("act", act)
            hgrn_act(act, st, r2), barrier("act", act)
            outp_act(act, 2, r2), barrier("act", act)
            ln_act(act)

        @block.vector
        def _(dve):
            dve.wait_ge(consts_in, CONSTS)
            st = Steps(dve, dve_step)
            for to, k0, k1 in ((tril4[:], 0, 4), (lmask[:], 4, 4 + LEVELS), (lmaskt[:], 4 + LEVELS, MASKS)):
                st(dve.tensor_copy(to.rearrange("p a n -> p (a n)") if k0 else to, masks[:, k0 * P:k1 * P]))
            norm_dve(dve, st, 0, r2, r1), barrier("dve", dve)
            forget_dve(dve, st), barrier("dve", dve)
            attn_dve(dve, st, "fox", r2), barrier("dve", dve)
            outp_dve(dve, 0, r2, r2_split, r1), barrier("dve", dve)
            norm_dve(dve, st, 1, r1, r2), barrier("dve", dve)
            attn_dve(dve, st, "swa", r1), barrier("dve", dve)
            outp_dve(dve, 1, r1, r1_split, r2), barrier("dve", dve)
            norm_dve(dve, st, 2, r2, r1), barrier("dve", dve)
            wa_dve(dve, st)
            rwkv_dve(dve, st, r2), barrier("dve", dve)
            hgrn_dve(dve, st, r2), barrier("dve", dve)
            outp_dve(dve, 2, r2, r2_split, r1), barrier("dve", dve)
            ln_dve(dve, st, r1)

        @block.gpsimd
        def _(pool):
            st = Steps(pool, pool_step)
            norm_pool(pool, 0, r2), barrier("pool", pool)
            forget_pool(pool), barrier("pool", pool)
            attn_pool(pool, st, "fox"), barrier("pool", pool)
            outp_pool(pool, 0), barrier("pool", pool)
            norm_pool(pool, 1, r1), barrier("pool", pool)
            attn_pool(pool, st, "swa"), barrier("pool", pool)
            outp_pool(pool, 1), barrier("pool", pool)
            norm_pool(pool, 2, r2), barrier("pool", pool)
            wa_pool(pool)
            rwkv_pool(pool), barrier("pool", pool)
            hgrn_pool(pool), barrier("pool", pool)
            outp_pool(pool, 2), barrier("pool", pool)
            ln_pool(pool)


def kernel(**inputs):
    import concourse.bacc as bacc
    from concourse.bass_utils import run_bass_kernel_spmd
    import ml_dtypes

    x = {k: np.asarray(v) for k, v in inputs.items()}

    def slots(w, width):
        per = 4 * N // width
        k, n = w.shape
        v = w.reshape(KT // per, per, P, n // width, width).transpose(3, 0, 2, 1, 4)
        return v.reshape(-1, P, 4 * N)

    def by_round(ws, width):
        parts = [slots(w, width).reshape(w.shape[1] // width, -1, P, 4 * N) for w in ws]
        return np.concatenate(parts, axis=1).reshape(-1, P, 4 * N)

    def rows(v, n=P):
        return np.ascontiguousarray(v.reshape(-1, n).T)

    fw, sw, w2 = x["fox_w_in"][0], x["swa_w_in"][0], x["w_in_2"][0]
    kv0 = D + GROUPS * HD
    lo, hi = 4 * RW, 4 * RW + 2 * RANK
    stream = np.concatenate([
        by_round([fw[:, j * D:(j + 1) * D] for j in range(4)], N),
        slots(x["fox_w_out"][0], N),
        by_round([sw[:, 0:D], sw[:, D + 2 * GROUPS * HD:]], N),
        slots(x["swa_w_out"][0], N),
        by_round([w2[:, j * RW:(j + 1) * RW] for j in range(4)], HALF),
        by_round([w2[:, hi + j * RW:hi + (j + 1) * RW] for j in range(4)], HALF),
        slots(x["w_out_2"][0], N)])
    assert stream.shape[0] == ALL_SLOTS
    w_kv = np.stack([np.concatenate([sw[:, D + g * HD:D + (g + 1) * HD], sw[:, kv0 + g * HD:kv0 + (g + 1) * HD]], 1)
                     .reshape(KT, P, P).transpose(1, 0, 2) for g in range(GROUPS)])
    mu = x["shift_mu_2"][0]

    def rounds(v):
        return v.reshape(ROUNDS_, HALF // P, P).transpose(0, 2, 1)

    ROUNDS_ = RW // HALF
    rw_mu = np.stack([rounds(mu[j * RW:(j + 1) * RW]) for j in range(4)], axis=-1)
    rw_par = np.stack([rounds(x[name][0]) for name in ("w_decay0_2", "a0_2", "k_k_2", "k_a_2", "r_k_2")], axis=-1)
    up = np.zeros((ROUNDS_, P, 2, HALF), np.float32)
    up[:, 0:RANK, 0, :] = x["w_decay_up_2"][0].reshape(RANK, ROUNDS_, HALF).transpose(1, 0, 2)
    up[:, RANK:P, 1, :] = x["a_up_2"][0].reshape(RANK, ROUNDS_, HALF).transpose(1, 0, 2)
    hg_par = np.stack([rounds(x["lb_logits_2"][0]), rounds(x["g_norm_w_2"][0])], axis=-1)

    later, earlier = np.arange(P)[:, None], np.arange(P)[None, :]
    levels = np.stack([(later >> (l + 1) == earlier >> (l + 1)) & (later >> l & 1 == 1) & (earlier >> l & 1 == 0)
                       for l in range(LEVELS)])
    upper, upper_eq = later < earlier, later <= earlier
    tril4 = np.concatenate([upper, upper_eq, upper, upper_eq], axis=1).astype(np.int32)
    lmask = levels.transpose(1, 0, 2).astype(np.int32)
    lmaskt = np.concatenate([levels.transpose(0, 2, 1), (later == earlier)[None]]).transpose(1, 0, 2).astype(np.int32)
    maskb = np.where(np.concatenate([earlier > later, earlier <= later], axis=1), 0.0, NEG).astype(ml_dtypes.bfloat16)
    inv = np.float32(500000.0) ** (-np.arange(ROT, dtype=np.float32) / np.float32(ROT))
    ang = (np.arange(SEQ, dtype=np.float32)[:, None] * inv[None, :]).astype(np.float64)
    bones = np.kron(np.eye(2), np.ones((HD, HD))).astype(np.float32)
    arrays = {
        "x": x["x"][0], "w": stream, "w_kv": w_kv,
        "gains": np.concatenate([x["norm_g"], x["final_g"][None]], 0),
        "w_f": fw[:, 4 * D:].reshape(KT, P, FOX_HEADS).transpose(1, 0, 2), "b_f": x["fox_b_f"].T,
        "sinks": x["swa_sinks"], "w_wa": w2[:, lo:hi].reshape(KT, P, P).transpose(1, 0, 2), "wa_mu": mu[lo:hi, None],
        "rw_par": rw_par, "rw_mu": rw_mu.transpose(1, 0, 2, 3).reshape(P, -1), "rw_up": up, "gn_w": x["ln_x_w_2"].reshape(ROUNDS_, HALF), "gn_b": x["ln_x_b_2"].reshape(ROUNDS_, HALF),
        "hg_par": hg_par, "ln": np.concatenate([x["ln_w_2"], x["ln_b_2"]], 0),
        "ident": np.eye(P, dtype=np.float32), "identb": np.eye(P).astype(ml_dtypes.bfloat16), "maskb": maskb,
        "masks": np.concatenate([m.reshape(P, -1) for m in (tril4, lmask, lmaskt)], 1),
        "eps": np.tile(np.array([[RMS_EPS, LN_EPS, GN_EPS, HGRN_EPS]], np.float32), (P, 1)),
        "cos": np.cos(ang).astype(np.float32).reshape(TT, P, ROT).transpose(1, 0, 2),
        "sin": np.sin(ang).astype(np.float32).reshape(TT, P, ROT).transpose(1, 0, 2),
        "bones": bones, "bones2": np.ascontiguousarray(bones[:, ::HD]),
        "reset": np.tile((np.arange(SEQ) % CH != 0).astype(np.float32)[None], (P, 1)),
    }
    nc = bacc.Bacc("TRN2", target_bir_lowering=False, num_devices=1, dynamic_dma_scratch_size=4096)
    a, given = {}, {}
    for name, v in arrays.items():
        v = np.ascontiguousarray(v)
        given[f"in_{name}"] = v
        a[name] = nc.dram_tensor(f"in_{name}", v.shape, mybir.dt.from_np(v.dtype), kind="ExternalInput").ap()
    a["x1"] = nc.dram_tensor("x1", [SEQ, D], F32).ap()
    a["x2"] = nc.dram_tensor("x2", [SEQ, D], F32).ap()
    a["c3"] = nc.dram_tensor("c3", [3, FOX_HEADS * SEQ], BF16).ap()
    out = nc.dram_tensor("out_0", [SEQ, D], F32, kind="ExternalOutput").ap()
    build(nc, a, out)
    r = run_bass_kernel_spmd(nc, [given], core_ids=[0])
    return r.results[0]["out_0"].reshape(1, SEQ, D)
```
